# Optimizing a Trainium2 kernel written in Bass

```python
import math
import jax, jax.numpy as jnp
from jax import lax
import numpy as np

D_MODEL = 1024
BATCH = 1
SEQ = 256
DEPTH = 2

N_MIXERS = 2
N_POOL_LAYERS = (DEPTH + 1) // 2
N_MOBA_LAYERS = DEPTH // 2
POOL_WINDOWS = (2, 4, 8, 16)
N_POOL_GROUPS = len(POOL_WINDOWS)
POOL_GROUP = D_MODEL // N_POOL_GROUPS
HEAD_DIM = 64
N_HEADS = D_MODEL // HEAD_DIM
MOBA_BLOCK = 256
MOBA_TOPK = 3
Q_CHUNK = 128
NUM_BUCKETS = 32
MAX_DISTANCE = 1024
D_FF = 4 * D_MODEL
EPS = 1e-6


def rmsnorm(x, g):
    xf = x.astype(jnp.float32)
    y = xf * lax.rsqrt(jnp.mean(xf * xf, axis=-1, keepdims=True) + EPS)
    return (y * g.astype(jnp.float32)).astype(x.dtype)

def modulate(h, shift, scale):
    return h * (1 + scale[:, None, :]) + shift[:, None, :]

def t5_bucket(dist):
    max_exact = NUM_BUCKETS // 2
    nf = jnp.maximum(dist, 1).astype(jnp.float32)
    large = max_exact + (jnp.log(nf / max_exact) / math.log(MAX_DISTANCE / max_exact)
                         * (NUM_BUCKETS - max_exact)).astype(jnp.int32)
    large = jnp.minimum(large, NUM_BUCKETS - 1)
    return jnp.where(dist < max_exact, dist, large)

def pool_mixer(h, w_pool, pool_scale):
    B, S, D = h.shape
    hf = h.astype(jnp.float32)
    cs = jnp.concatenate([jnp.zeros((B, 1, D), jnp.float32), jnp.cumsum(hf, axis=1)], axis=1)
    t = jnp.arange(S)
    groups = []
    for g, w in enumerate(POOL_WINDOWS):
        sl = slice(g * POOL_GROUP, (g + 1) * POOL_GROUP)
        cs_g = cs[:, :, sl]
        lo = jnp.maximum(t + 1 - w, 0)
        win_sum = cs_g[:, 1:] - jnp.take(cs_g, lo, axis=1)
        cnt = jnp.minimum(t + 1, w).astype(jnp.float32)[None, :, None]
        groups.append(win_sum / cnt - hf[:, :, sl])
    pooled = jnp.stack(groups, axis=2)
    y = jnp.einsum('bsgi,gio->bsgo', pooled, w_pool.astype(jnp.float32)).reshape(B, S, D)
    return (y * pool_scale.astype(jnp.float32)).astype(h.dtype)

def moba_attention(h, w_qkv, w_o, rel_bias):
    B, S, D = h.shape
    H, Dh, BL = N_HEADS, HEAD_DIM, MOBA_BLOCK
    qkv = h @ w_qkv
    q, k, v = jnp.split(qkv, 3, axis=-1)
    q = q.reshape(B, S, H, Dh).transpose(0, 2, 1, 3)
    k = k.reshape(B, S, H, Dh).transpose(0, 2, 1, 3)
    v = v.reshape(B, S, H, Dh).transpose(0, 2, 1, 3)
    nb = -(-S // BL)
    pad = nb * BL - S
    kb = jnp.pad(k, ((0, 0), (0, 0), (0, pad), (0, 0))).reshape(B, H, nb, BL, Dh)
    vb = jnp.pad(v, ((0, 0), (0, 0), (0, pad), (0, 0))).reshape(B, H, nb, BL, Dh)
    kmean = jnp.mean(kb.astype(jnp.float32), axis=3)
    top = min(MOBA_TOPK, nb - 1)
    scale = HEAD_DIM ** -0.5
    rb = rel_bias.astype(jnp.float32)
    rbT = rb.T
    bi = jnp.arange(B)[:, None, None]
    hi = jnp.arange(H)[None, :, None]
    hi4 = jnp.arange(H)[None, :, None, None]
    n_chunks = S // Q_CHUNK

    def chunk_fn(ci):
        s0 = ci * Q_CHUNK
        qf = lax.dynamic_slice_in_dim(q, s0, Q_CHUNK, axis=2).astype(jnp.float32)
        tq = s0 + jnp.arange(Q_CHUNK)
        own = s0 // BL
        k_own = lax.dynamic_index_in_dim(kb, own, axis=2, keepdims=False)
        v_own = lax.dynamic_index_in_dim(vb, own, axis=2, keepdims=False)
        dist_own = tq[:, None] - (own * BL + jnp.arange(BL))[None, :]
        bias_own = rb[t5_bucket(jnp.maximum(dist_own, 0))].transpose(2, 0, 1)[None]
        logit_own = jnp.einsum('bhqd,bhkd->bhqk', qf, k_own.astype(jnp.float32)) * scale + bias_own
        logit_own = jnp.where((dist_own >= 0)[None, None], logit_own, -jnp.inf)
        logits = []
        sel = []
        if top > 0:
            gate = jnp.einsum('bhqd,bhnd->bhqn', qf, kmean)
            past = jnp.arange(nb) < own
            gate = jnp.where(past[None, None, None], gate, -jnp.inf)
            _, idx = lax.top_k(gate, top)
            for r in range(top):
                idx_r = idx[..., r]
                k_sel = kb[bi, hi, idx_r]
                kpos = idx_r[..., None] * BL + jnp.arange(BL)
                dist = tq[None, None, :, None] - kpos
                bias_r = rbT[hi4, t5_bucket(jnp.maximum(dist, 0))]
                lg = jnp.einsum('bhqd,bhqkd->bhqk', qf, k_sel.astype(jnp.float32)) * scale + bias_r
                lg = jnp.where((idx_r < own)[..., None], lg, -jnp.inf)
                logits.append(lg)
                sel.append(idx_r)
        logits.append(logit_own)
        p = jax.nn.softmax(jnp.concatenate(logits, axis=-1), axis=-1)
        out = jnp.einsum('bhqk,bhkd->bhqd', p[..., top * BL:], v_own.astype(jnp.float32))
        for r in range(top):
            v_sel = vb[bi, hi, sel[r]]
            out = out + jnp.einsum('bhqk,bhqkd->bhqd', p[..., r * BL:(r + 1) * BL],
                                   v_sel.astype(jnp.float32))
        return out.astype(h.dtype)

    o = lax.map(chunk_fn, jnp.arange(n_chunks))
    o = o.transpose(1, 0, 3, 2, 4).reshape(B, S, D)
    return o @ w_o

def squared_relu_mlp(h, w_up, w_down):
    a = jax.nn.relu(h @ w_up)
    return (a * a) @ w_down

def first_inputs(seed: int = 0) -> dict:
    key = jax.random.key(seed)
    ks = jax.random.split(key, 16)
    f32 = jnp.float32
    D = D_MODEL
    nrm = lambda k, shape, s: jax.random.normal(k, shape, f32) * s
    return {
        "x": nrm(ks[0], (BATCH, SEQ, D), 1.0),
        "c": nrm(ks[1], (BATCH, D), 1.0),
        "rel_bias": nrm(ks[2], (NUM_BUCKETS, N_HEADS), 0.5),
        "w_mod": nrm(ks[3], (DEPTH, D, 6 * D), 0.5 * D ** -0.5),
        "b_mod": nrm(ks[4], (DEPTH, 6 * D), 0.02),
        "norm_mix": 1.0 + nrm(ks[5], (DEPTH, D), 0.02),
        "norm_mlp": 1.0 + nrm(ks[6], (DEPTH, D), 0.02),
        "w_pool": nrm(ks[7], (N_POOL_LAYERS, N_POOL_GROUPS, POOL_GROUP, POOL_GROUP), POOL_GROUP ** -0.5),
        "pool_scale": 1.0 + nrm(ks[8], (N_POOL_LAYERS, D), 0.05),
        "w_qkv": nrm(ks[9], (N_MOBA_LAYERS, D, 3 * D), D ** -0.5),
        "w_o": nrm(ks[10], (N_MOBA_LAYERS, D, D), D ** -0.5),
        "w_up": nrm(ks[11], (DEPTH, D, D_FF), D ** -0.5),
        "w_down": nrm(ks[12], (DEPTH, D_FF, D), D_FF ** -0.5),
        "norm_final": 1.0 + nrm(ks[13], (D,), 0.02),
    }

def first_block(x, c, rel_bias, w_mod, b_mod, norm_mix, norm_mlp, w_pool, pool_scale,
              w_qkv, w_o, w_up, w_down, norm_final):
    c_act = jax.nn.silu(c)
    for i in range(DEPTH):
        mod = c_act @ w_mod[i] + b_mod[i]
        sh1, sc1, g1, sh2, sc2, g2 = jnp.split(mod, 6, axis=-1)
        h = modulate(rmsnorm(x, norm_mix[i]), sh1, sc1)
        if i % N_MIXERS == 0:
            y = pool_mixer(h, w_pool[i // N_MIXERS], pool_scale[i // N_MIXERS])
        else:
            y = moba_attention(h, w_qkv[i // N_MIXERS], w_o[i // N_MIXERS], rel_bias)
        x = x + g1[:, None, :] * y
        h = modulate(rmsnorm(x, norm_mlp[i]), sh2, sc2)
        x = x + g2[:, None, :] * squared_relu_mlp(h, w_up[i], w_down[i])
    return rmsnorm(x, norm_final)


DEPTH_2 = 1

D_CONV = 1024
CONV_K = 31
D_RNN = 1280
LRU_HEADS = 16
LRU_BLOCK = D_RNN // LRU_HEADS
LRU_CONV_K = 4
LRU_C = 8.0
D_FF_2 = ((int(math.ceil(8 * D_MODEL / 3)) + 255) // 256) * 256
IN_SPLITS = (2 * D_CONV, D_RNN, D_RNN, D_MODEL, D_MODEL)
D_IN = sum(IN_SPLITS)


def rmsnorm_2(x, g):
    xf = x.astype(jnp.float32)
    y = xf * lax.rsqrt(jnp.mean(xf * xf, axis=-1, keepdims=True) + EPS)
    return (y * g.astype(jnp.float32)).astype(x.dtype)

def layernorm(x, g, b):
    xf = x.astype(jnp.float32)
    mu = jnp.mean(xf, axis=-1, keepdims=True)
    xc = xf - mu
    var = jnp.mean(xc * xc, axis=-1, keepdims=True)
    y = xc * lax.rsqrt(var + EPS) * g.astype(jnp.float32) + b.astype(jnp.float32)
    return y.astype(x.dtype)

def causal_depthwise_conv(u, w, b):
    k, c = w.shape
    u_pad = jnp.pad(u, ((0, 0), (k - 1, 0), (0, 0)))
    y = lax.conv_general_dilated(
        u_pad, w[:, None, :].astype(u.dtype), window_strides=(1,), padding='VALID',
        dimension_numbers=('NWC', 'WIO', 'NWC'), feature_group_count=c)
    return y + b.astype(u.dtype)

def _linear_recurrence_combine(left, right):
    a1, b1 = left
    a2, b2 = right
    return a1 * a2, a2 * b1 + b2

def rg_lru(xb, wa, ba, wx, bx, lam):
    bsz, s, d = xb.shape
    xf = xb.astype(jnp.float32)
    xh = xf.reshape(bsz, s, LRU_HEADS, LRU_BLOCK)
    r = jax.nn.sigmoid(jnp.einsum('bshi,hij->bshj', xh, wa.astype(jnp.float32)).reshape(bsz, s, d)
                       + ba.astype(jnp.float32))
    i = jax.nn.sigmoid(jnp.einsum('bshi,hij->bshj', xh, wx.astype(jnp.float32)).reshape(bsz, s, d)
                       + bx.astype(jnp.float32))
    log_a = -LRU_C * r * jax.nn.softplus(-lam.astype(jnp.float32))
    a = jnp.exp(log_a)
    mult = jnp.sqrt(-jnp.expm1(2.0 * log_a))
    bterm = mult * (i * xf)
    _, h = lax.associative_scan(_linear_recurrence_combine, (a, bterm), axis=1)
    return h.astype(xb.dtype)

def second_inputs(seed: int = 0) -> dict:
    key = jax.random.key(seed)
    ks = jax.random.split(key, 32)
    f32 = jnp.float32
    L = DEPTH_2

    def nrm(k, shape, fan_in, scale=1.0):
        return jax.random.normal(k, shape, f32) * (scale * fan_in ** -0.5)

    def small(k, shape, s=0.02):
        return jax.random.normal(k, shape, f32) * s

    x = jax.random.normal(ks[0], (BATCH, SEQ, D_MODEL), f32)
    a0 = jax.random.uniform(ks[16], (L, D_RNN), f32, 0.9, 0.999)
    lru_lambda = jnp.log(a0) - jnp.log1p(-a0)
    return {
        "x": x,
        "norm1_g": 1.0 + small(ks[1], (L, D_MODEL)),
        "w_in": nrm(ks[2], (L, D_MODEL, D_IN), D_MODEL),
        "b_in": small(ks[3], (L, D_IN)),
        "conv_dw_w": nrm(ks[4], (L, CONV_K, D_CONV), CONV_K),
        "conv_dw_b": small(ks[5], (L, D_CONV)),
        "conv_ln_g": 1.0 + small(ks[6], (L, D_CONV)),
        "conv_ln_b": small(ks[7], (L, D_CONV)),
        "conv_w_out": nrm(ks[8], (L, D_CONV, D_MODEL), D_CONV),
        "conv_b_out": small(ks[9], (L, D_MODEL)),
        "lru_conv_w": nrm(ks[10], (L, LRU_CONV_K, D_RNN), LRU_CONV_K),
        "lru_conv_b": small(ks[11], (L, D_RNN)),
        "lru_wa": nrm(ks[12], (L, LRU_HEADS, LRU_BLOCK, LRU_BLOCK), LRU_BLOCK),
        "lru_ba": small(ks[13], (L, D_RNN)),
        "lru_wx": nrm(ks[14], (L, LRU_HEADS, LRU_BLOCK, LRU_BLOCK), LRU_BLOCK),
        "lru_bx": small(ks[15], (L, D_RNN)),
        "lru_lambda": lru_lambda,
        "lru_w_out": nrm(ks[17], (L, D_RNN, D_MODEL), D_RNN),
        "w_mix_out": nrm(ks[18], (L, D_MODEL, D_MODEL), D_MODEL),
        "norm2_g": 1.0 + small(ks[19], (L, D_MODEL)),
        "ffn_w1": nrm(ks[20], (L, D_MODEL, D_FF_2), D_MODEL),
        "ffn_w3": nrm(ks[21], (L, D_MODEL, D_FF_2), D_MODEL),
        "ffn_w2": nrm(ks[22], (L, D_FF_2, D_MODEL), D_FF_2),
        "norm_f_g": 1.0 + small(ks[23], (D_MODEL,)),
    }

def second_block(x, norm1_g, w_in, b_in, conv_dw_w, conv_dw_b, conv_ln_g, conv_ln_b,
              conv_w_out, conv_b_out, lru_conv_w, lru_conv_b, lru_wa, lru_ba, lru_wx,
              lru_bx, lru_lambda, lru_w_out, w_mix_out, norm2_g, ffn_w1, ffn_w3, ffn_w2,
              norm_f_g):
    split_idx = list(np.cumsum(IN_SPLITS)[:-1])
    for l in range(DEPTH_2):
        h = rmsnorm_2(x, norm1_g[l])
        z = h @ w_in[l] + b_in[l]
        z_glu, z_rx, z_rg, z_ga, z_gb = jnp.split(z, split_idx, axis=-1)

        u = z_glu[..., :D_CONV] * jax.nn.sigmoid(z_glu[..., D_CONV:])
        u = causal_depthwise_conv(u, conv_dw_w[l], conv_dw_b[l])
        u = jax.nn.silu(layernorm(u, conv_ln_g[l], conv_ln_b[l]))
        y_a = u @ conv_w_out[l] + conv_b_out[l]

        xb = causal_depthwise_conv(z_rx, lru_conv_w[l], lru_conv_b[l])
        hb = rg_lru(xb, lru_wa[l], lru_ba[l], lru_wx[l], lru_bx[l], lru_lambda[l])
        y_b = (hb * jax.nn.gelu(z_rg, approximate=True)) @ lru_w_out[l]

        m = jax.nn.sigmoid(z_ga) * y_a + jax.nn.sigmoid(z_gb) * y_b
        x = x + m @ w_mix_out[l]

        h = rmsnorm_2(x, norm2_g[l])
        x = x + (jax.nn.silu(h @ ffn_w1[l]) * (h @ ffn_w3[l])) @ ffn_w2[l]
    return rmsnorm_2(x, norm_f_g)


def setup_inputs(seed=0):
    out = dict(first_inputs(seed))
    for name, value in second_inputs(seed + 1).items():
        if name != "x":
            out[name + "_2"] = value
    return out


def reference(
    x, c, rel_bias, w_mod, b_mod, norm_mix, norm_mlp, w_pool, pool_scale, w_qkv, w_o, w_up,
    w_down, norm_final, norm1_g_2, w_in_2, b_in_2, conv_dw_w_2, conv_dw_b_2, conv_ln_g_2,
    conv_ln_b_2, conv_w_out_2, conv_b_out_2, lru_conv_w_2, lru_conv_b_2, lru_wa_2, lru_ba_2,
    lru_wx_2, lru_bx_2, lru_lambda_2, lru_w_out_2, w_mix_out_2, norm2_g_2, ffn_w1_2, ffn_w3_2,
    ffn_w2_2, norm_f_g_2,
):
    x = first_block(
        x, c, rel_bias, w_mod, b_mod, norm_mix, norm_mlp, w_pool, pool_scale, w_qkv, w_o, w_up,
        w_down, norm_final,
    )
    return second_block(
        x, norm1_g_2, w_in_2, b_in_2, conv_dw_w_2, conv_dw_b_2, conv_ln_g_2, conv_ln_b_2,
        conv_w_out_2, conv_b_out_2, lru_conv_w_2, lru_conv_b_2, lru_wa_2, lru_ba_2, lru_wx_2,
        lru_bx_2, lru_lambda_2, lru_w_out_2, w_mix_out_2, norm2_g_2, ffn_w1_2, ffn_w3_2,
        ffn_w2_2, norm_f_g_2,
    )


_drawn_inputs = setup_inputs


def setup_inputs(seed=0):
    import zlib

    import numpy as np

    out = dict(_drawn_inputs(seed))
    spreads = {}
    factors = {'norm_mix': 7.384,
     'norm_mlp': 3.835,
     'pool_scale': 3.608,
     'norm1_g_2': 4.959,
     'b_in_2': 3.388,
     'conv_dw_b_2': 12.495,
     'conv_ln_g_2': 142.965,
     'conv_ln_b_2': 132.477,
     'conv_b_out_2': 92.867,
     'lru_conv_b_2': 12.586,
     'lru_ba_2': 55.546,
     'lru_bx_2': 46.045,
     'norm2_g_2': 17.816,
     'norm_f_g_2': 23.239}
    for name, (base, spread) in spreads.items():
        noise = np.random.default_rng([zlib.crc32(name.encode()), seed]).standard_normal(out[name].shape)
        drawn = base * np.exp(spread * noise) if base else spread * noise
        out[name] = __import__('jax').numpy.asarray(drawn.astype(out[name].dtype))
    for name, factor in factors.items():
        out[name] = (out[name] * factor).astype(out[name].dtype)
    return out
```

```python
from contextlib import ExitStack, contextmanager
import math

import numpy as np

import concourse.bass as bass
from concourse import mybir

ALU = mybir.AluOpType
ACT = mybir.ActivationFunctionType
AX = mybir.AxisListType
F32 = mybir.dt.float32
F32R = mybir.dt.float32r

P = 128
SEQ = 256
D = 1024
DC = D // P
FFC = 4 * D // P
RC = 1280 // P
F2C = 2816 // P
HEADS, HD = 16, 64
EPS = 1e-6
WINDOWS = (2, 4, 8, 16)
TAPS, RTAPS = 31, 4
UT = 8
PAIR = 2 * UT * P
RAW = 4
HL = 4
LEAD = 3

PHASES = [("pool", 2, 8), ("up0", 32, 32), ("down0", 32, 8), ("qkv", 24, 24), ("o", 8, 8),
          ("up1", 32, 32), ("down1", 32, 8), ("rx", 10, 10), ("glu", 16, 16), ("rg", 10, 10),
          ("gates", 8, 20), ("gb", 8, 8), ("ga", 8, 8), ("lru", 10, 8), ("conv", 8, 8),
          ("mix", 8, 8), ("ffn", 44, 44), ("w2", 22, 8)]
U0, T0, N_UNITS, n = {}, {}, 0, 0
for _name, _u, _t in PHASES:
    U0[_name], T0[_name] = N_UNITS, n
    N_UNITS += _u
    n += _t if _name != "gates" else 0
N_PAIRS = N_UNITS // 2

SC1, SH1, G1, SC2, SH2, G2 = range(6)
MOD_ORDER = (1, 0, 2, 4, 3, 5)
MODS = 48
MOD_FIRST = 20

VEC = {}


def _columns():
    at = 0
    for name, k in (("c", DC), ("b_mod", 96), ("norm_mix", 16), ("norm_mlp", 16), ("pool_scale", 8),
                    ("norm_final", 8), ("norm1", 8), ("norm2", 8), ("norm_f", 8), ("b_in", 52),
                    ("dw_w", TAPS * DC), ("dw_b", DC), ("ln_g", DC), ("ln_b", DC), ("cb", DC),
                    ("rw", RTAPS * RC), ("rb", RC), ("ba", RC), ("bx", RC), ("lam", RC)):
        VEC[name] = at
        at += k
    return at


NVEC = _columns()


def gate_tiles():
    return [sorted({r // P for h in range(m * P // 80, (m * P + P - 1) // 80 + 1)
                    for r in range(80 * h, 80 * h + 80)}) for m in range(RC)]


def gate_stream():
    out = []
    for m, ks in enumerate(gate_tiles()):
        for which in range(2):
            out += [(m, which, k, k == ks[0], k == ks[-1]) for k in ks]
    return out


GATES = gate_stream()
GATE_UNITS = 8
GATE_AT = [(n * GATE_UNITS // len(GATES),
            n - sum(t * GATE_UNITS // len(GATES) < n * GATE_UNITS // len(GATES) for t in range(len(GATES))))
           for n in range(len(GATES))]
GATE_DONE = [GATE_AT[n][0] for n, g in enumerate(GATES) if g[4]]


def mod_slot(q):
    return q % 4 if q < MOD_FIRST else q % 2


def mod_landed(q):
    return 16 * sum(mod_slot(r) == mod_slot(q) for r in range(q + 1))


def build(nc, weights, w_mod, x_in, vectors, rel_bias, buckets, inv_count, identity, out):
    scratch = nc.dram_tensor("bias_by_distance", [HEADS, 384], F32, kind="Internal").ap()
    with ExitStack() as ctx:
        def sb(name, shape, dt=F32, where=ctx):
            return where.enter_context(nc.sbuf_tensor(name, shape, dt))

        def sem(name):
            return ctx.enter_context(nc.semaphore(name))

        raw = sb("raw", [P, RAW, PAIR])
        w_hi = sb("w_hi", [P, HL, UT * P], F32R)
        w_lo = sb("w_lo", [P, HL, UT * P], F32R)
        x = sb("x", [P, DC, SEQ])
        xg_hi = sb("xg_hi", [P, DC, SEQ + 2], F32R)
        xg_lo = sb("xg_lo", [P, DC, SEQ + 2], F32R)
        vec = sb("vec", [P, NVEC])
        modv = sb("modv", [P, 96])
        gain = sb("gain", [P, 4, DC])
        gate0 = sb("gate0", [P, DC])
        gain1 = sb("gain1", [P, DC])
        ones = sb("ones", [P, P])
        ident = sb("ident", [P, P])
        rstd = sb("rstd", [P, SEQ + 2])
        rstd1 = sb("rstd1", [P, SEQ])
        var = sb("var", [P, SEQ])
        newt = sb("newt", [P, 2, SEQ])
        acc = sb("acc", [P, SEQ])
        acc2 = sb("acc2", [P, SEQ])
        sq = sb("sq", [P, 2, SEQ])
        ab = sb("ab", [P, 2, SEQ + 2])
        sp = sb("sp", [P, 8, RC])
        eps = sb("eps", [P, 1])

        first = ExitStack()
        cz = sb("cz", [P, DC, 32], F32, first)
        mod_raw = sb("mod_raw", [P, 4, DC * SEQ], F32, first)
        mod_row = sb("mod_row", [P, 2, SEQ], F32, first)
        ub = sb("ub", [P, 2, SEQ], F32, first)
        sb2 = sb("sb2", [P, 2, SEQ], F32, first)
        with ExitStack() as part:
            PADW = SEQ + 16
            h_pad = sb("h_pad", [P, DC, PADW], F32, part)
            s2 = sb("s2", [P, DC, PADW], F32, part)
            s4 = sb("s4", [P, 6, PADW], F32, part)
            s8 = sb("s8", [P, 4, PADW], F32, part)
            s16 = sb("s16", [P, 2, PADW], F32, part)
            invc = sb("invc", [P, 4, SEQ], F32, part)
            rbx = sb("rbx", [33, HEADS], F32, part)
            bkt = sb("bkt", [33, 384], F32, part)
            bydist = sb("bydist", [HEADS, 384], F32, part)
            pool_hi = sb("pool_hi", [P, DC, SEQ], F32R, part)
            pool_lo = sb("pool_lo", [P, DC, SEQ], F32R, part)
        with ExitStack() as part:
            hid_hi = sb("hid_hi", [P, FFC, SEQ], F32R, part)
            hid_lo = sb("hid_lo", [P, FFC, SEQ], F32R, part)
        with ExitStack() as part:
            qT = sb("qT", [P, 2, SEQ], F32, part)
            kT = sb("kT", [P, 2, SEQ], F32, part)
            vT = sb("vT", [P, 2, SEQ], F32, part)
            vtok = sb("vtok", [P, 2, SEQ], F32, part)
            toep = sb("toep", [P, 2, 2, 384], F32, part)
            logit = sb("logit", [P, 2, 384], F32, part)
            prob = sb("prob", [P, 2, 384], F32, part)
            probn = sb("probn", [P, 2, 384], F32, part)
            pT = sb("pT", [P, 2, 384], F32, part)
            smx = sb("smx", [P, 2, 8], F32, part)
            o_hi = sb("o_hi", [P, DC, SEQ], F32R, part)
            o_lo = sb("o_lo", [P, DC, SEQ], F32R, part)
        first.close()
        with ExitStack() as part:
            RXW = SEQ + RTAPS - 1
            UW = SEQ + TAPS - 1
            rx = sb("rx", [P, RC, RXW], F32, part)
            act_hi = sb("act_hi", [P, RC, SEQ], F32R, part)
            act_lo = sb("act_lo", [P, RC, SEQ], F32R, part)
            u = sb("u", [P, DC, UW], F32, part)
            y = sb("y", [P, DC, SEQ], F32, part)
            grg = sb("grg", [P, RC, SEQ], F32, part)
            rt = sb("rt", [P, RC, SEQ], F32, part)
            ig = sb("ig", [P, RC, SEQ], F32, part)
            av = sb("av", [P, RC, SEQ], F32, part)
            sga = sb("sga", [P, DC, SEQ], F32, part)
            sgb = sb("sgb", [P, DC, SEQ], F32, part)
        with ExitStack() as part:
            f_hi = sb("f_hi", [P, F2C, SEQ], F32R, part)
            f_lo = sb("f_lo", [P, F2C, SEQ], F32R, part)
            yout = sb("yout", [P, DC, SEQ], F32, part)

        banks = [ctx.enter_context(nc.psum_tensor(f"bank{b}", [P, 512], F32)) for b in range(8)]
        row_bank, col_banks, stat_bank, s_bank, t_bank, o_bank = banks[4], (banks[5], banks[7]), banks[6], banks[6], banks[7], banks[3]

        landed = [sem(f"landed{k}") for k in range(RAW)]
        hi_done = sem("hi_done")
        lo_done = sem("lo_done")
        pe_units = sem("pe_units")
        tile_read = sem("tile_read")
        mod_in = [sem(f"mod_in{k}") for k in range(4)]
        mod_rows = sem("mod_rows")
        mod_copied = sem("mod_copied")
        mod_cols = sem("mod_cols")
        mod_read = sem("mod_read")
        x_in_s, vec_in, small_in, inv_in = sem("x_in_s"), sem("vec_in"), sem("small_in"), sem("inv_in")
        consts = sem("consts")
        pads = sem("pads")
        c_act = sem("c_act")
        x_sq = sem("x_sq")
        dve = sem("dve_chain")
        stat_in = sem("stat_in")
        stat_mm = sem("stat_mm")
        var_done = sem("var_done")
        root_done = sem("root_done")
        rstd_done = sem("rstd_done")
        gain_done = sem("gain_done")
        xr_done = sem("xr_done")
        h_done = sem("h_done")
        pool_in = sem("pool_in")
        shift_done = sem("shift_done")
        sq_done = sem("sq_done")
        acc_done = sem("acc_done")
        acc2_done = sem("acc2_done")
        xg_hi_done = sem("xg_hi_done")
        xg_lo_done = sem("xg_lo_done")
        relu_done = sem("relu_done")
        sq2_done = sem("sq2_done")
        hid_hi_done = sem("hid_hi_done")
        hid_lo_done = sem("hid_lo_done")
        bias_mm, bias_cp, bias_out = sem("bias_mm"), sem("bias_cp"), sem("bias_out")
        toep_in = [sem("toep_in0"), sem("toep_in1")]
        qkv_done = sem("qkv_done")
        score_done = sem("score_done")
        logit_done = sem("logit_done")
        max_done = sem("max_done")
        neg_done = sem("neg_done")
        exp_done = sem("exp_done")
        prob_done = sem("prob_done")
        pt_done = sem("pt_done")
        pt_copied = sem("pt_copied")
        vt_done = sem("vt_done")
        vt_copied = sem("vt_copied")
        pv_done = sem("pv_done")
        o_hi_done = sem("o_hi_done")
        o_lo_done = sem("o_lo_done")
        z_done = sem("z_done")
        xb_done = sem("xb_done")
        act_hi_done = sem("act_hi_done")
        act_lo_done = sem("act_lo_done")
        u_done = sem("u_done")
        tap_done = sem("tap_done")
        gate_read = sem("gate_read")
        decay_done = sem("decay_done")
        mult2_done = sem("mult2_done")
        mult_done = sem("mult_done")
        hb_done = sem("hb_done")
        ln_sq, ln_silu, ln_hi, ln_lo = sem("ln_sq"), sem("ln_silu"), sem("ln_hi"), sem("ln_lo")
        ln_c, ln_n = sem("ln_c"), sem("ln_n")
        m_done = sem("m_done")
        f_silu, f_prod, f_hi_done, f_lo_done = sem("f_silu"), sem("f_prod"), sem("f_hi_done"), sem("f_lo_done")
        yout_done, stored = sem("yout_done"), sem("stored")

        def col(name, k, n=1):
            return vec[:, VEC[name] + k:VEC[name] + k + n]

        def loop_units(eng, name, step, end=None):
            n = PHASES[[p[0] for p in PHASES].index(name)][1] if end is None else end
            full = n // 8
            if full > 1:
                with eng.Fori(0, full) as i:
                    for j in range(8):
                        step(i, j)
                tail = range(8 * full, n)
            else:
                tail = range(n)
            for v in tail:
                step(v // 8, v % 8)

        def out_bank(name, v):
            if name in ("down0", "down1"):
                return banks[v % 2]
            if name == "qkv":
                return banks[v % 3]
            if name == "w2":
                return banks[v]
            if name == "gates":
                return banks[v % 4]
            return banks[(T0[name] + v) % 4]

        def one(i, k=1):
            return bass.ds(i, k) if not isinstance(i, int) else slice(i, i + k)

        def chunk(t, i, w=SEQ):
            return t[:, one(i), 0:w].rearrange("p a n -> p (a n)")

        def reverse(t):
            step, count = t.ap[0]
            return bass.AP(t.tensor, t.offset + P - 1, [[step, count], [P, 2], [-1, P]])

        block = ctx.enter_context(nc.Block())

        @block.sync
        def _(sp):
            sp.dma_start(x[:], x_in).then_inc(x_in_s, 16)
            sp.dma_start(vec[:], vectors).then_inc(vec_in, 16)

            def piece(q, s):
                if not isinstance(q, int) or q >= 4:
                    sp.wait_ge(mod_rows, q - (3 if isinstance(q, int) and q < MOD_FIRST else 1))
                sp.dma_start(mod_raw[:, s, :], w_mod[one(q)].rearrange("a p n -> p (a n)")).then_inc(mod_in[s], 16)

            def pair(p, s):
                if not isinstance(p, int) or p >= RAW:
                    sp.wait_ge(lo_done, 2 * (p - RAW) + 2)
                sp.dma_start(raw[:, s, :], weights[one(p)].rearrange("a p n -> p (a n)")).then_inc(landed[s], 16)

            for q in range(4):
                piece(q, q)
            sp.dma_start(rbx[0:32, :], rel_bias).then_inc(small_in, 16)
            sp.dma_start(bkt[:], buckets).then_inc(small_in, 16)
            sp.dma_start(ident[:], identity).then_inc(small_in, 16)
            sp.dma_start(invc[:], bass.AP(inv_count.tensor, 0, [[0, P], [SEQ, 4], [1, SEQ]])).then_inc(inv_in, 16)
            for q in range(4, 12):
                piece(q, mod_slot(q))
            pair(0, 0)
            sp.wait_ge(bias_cp, 1)
            sp.dma_start(scratch, bydist[:]).then_inc(bias_out, 16)
            for q in range(12, MOD_FIRST):
                piece(q, mod_slot(q))
            def mlp_loads(i):
                for s in range(4):
                    pair(4 * i + 1 + s, (1 + s) % RAW)
                    if s >= 2:
                        piece(2 * i + MOD_FIRST + s - 2, s - 2)

            mlp_loads(0)
            with sp.Fori(1, 8) as i:
                mlp_loads(i)

            def toeplitz(a):
                if a >= 2:
                    sp.wait_ge(logit_done, 2 * (a - 2) + 2)
                for seg, base in ((slice(0, 128), 128), (slice(128, 384), 0)):
                    src = bass.AP(scratch.tensor, base + 2 * 384 * a,
                                  [[1, P], [384, 2], [1, seg.stop - seg.start]])
                    sp.dma_start(toep[:, a % 2, :, seg], src).then_inc(toep_in[a % 2], 16)

            sp.wait_ge(bias_out, 16)
            p0 = U0["qkv"] // 2
            for n in range(12):
                pair(p0 + n, (p0 + n) % RAW)
                if n == 3:
                    sp.wait_ge(pe_units, U0["qkv"])
                for a in range(DC):
                    if n == max(3, min(11, (3 * a + 1) // 2 + 1)):
                        toeplitz(a)
                for q in range(DC):
                    if n == max(1, (3 * q - 2) // 2 + 1):
                        piece(36 + q, q % 2)
            for a in range(4):
                pair(p0 + 12 + a, (p0 + 12 + a) % RAW)
                piece(44 + a, a % 2)
            p0 += 16
            with sp.Fori(0, (N_PAIRS - p0) // RAW) as i:
                for s in range(RAW):
                    pair(4 * i + p0 + s, (p0 + s) % RAW)
            for m in range(DC):
                sp.wait_ge(yout_done, m + 1)
                sp.dma_start(out[m * P:(m + 1) * P, :], yout[:, m, :]).then_inc(stored, 16)
            sp.wait_ge(stored, 16 * DC)

        @block.gpsimd
        def _(pool):
            nc.gpsimd.memset(cz[:], 0.0).then_inc(consts, 1)
            nc.gpsimd.memset(ones[:], 1.0).then_inc(consts, 1)
            nc.gpsimd.memset(eps[:], EPS).then_inc(consts, 1)
            nc.gpsimd.memset(rstd[:, SEQ:SEQ + 2], 1.0).then_inc(consts, 1)
            pool.wait_ge(consts, 4)
            nc.gpsimd.memset(rbx[32:33, :], -1e30).then_inc(consts, 1)
            pool.wait_ge(consts, 5)
            for t in (h_pad, s2, s4, s8):
                nc.gpsimd.memset(t[:, :, 0:16], 0.0).then_inc(consts, 1)
            pool.wait_ge(pe_units, U0["rx"])
            nc.gpsimd.memset(rx[:, :, 0:RTAPS - 1], 0.0).then_inc(pads, 1)
            nc.gpsimd.memset(u[:, :, 0:TAPS - 1], 0.0).then_inc(pads, 1)

        @block.tensor
        def _(pe):
            def product(dst, slot, s, r_hi, r_lo, start, stop):
                hi = w_hi[:, slot, s * P:(s + 1) * P]
                lo = w_lo[:, slot, s * P:(s + 1) * P]
                pe.matmul(dst, hi, r_hi, start=start, stop=False, skip_group_check=True)
                pe.matmul(dst, hi, r_lo, start=False, stop=False, skip_group_check=True)
                return pe.matmul(dst, lo, r_hi, start=False, stop=stop, skip_group_check=True)

            def unit_ready(name, i, j):
                pe.wait_ge(hi_done, 8 * i + (U0[name] + j + 1))
                pe.wait_ge(lo_done, 8 * i + (U0[name] + j + 1))

            def rows(q, s, ready):
                pe.wait_ge(mod_in[s], ready)
                if not isinstance(q, int) or q > 0:
                    pe.wait_ge(mod_copied, q)
                for k in range(DC):
                    g = k % 4
                    mm = pe.matmul(row_bank[32 * g:32 * g + 32, 0:SEQ], cz[:, k, :], mod_raw[:, s, SEQ * k:SEQ * (k + 1)],
                                   start=k < 4, stop=k >= 4, tile_position=(0, 32 * g))
                mm.then_inc(mod_rows, 1)

            def cols(q, s):
                pe.wait_ge(mod_copied, q + 1)
                if isinstance(q, int) and q < MOD_FIRST:
                    g = q // 4
                    dst, at = col_banks[g % 2], 2 * (q % 4)
                    if g >= 2:
                        pe.wait_ge(mod_read, g - 1)
                else:
                    dst, at = col_banks[0], 0
                    pe.wait_ge(mod_read, q - (MOD_FIRST - 5))
                for half in range(2):
                    mm = pe.matmul(dst[:, at + half:at + half + 1], mod_row[:, s, half * P:(half + 1) * P],
                                   ones[:, 0:1], start=True, stop=True)
                mm.then_inc(mod_cols, 1)

            def stats(ready, src, at=0, dst=stat_bank):
                pe.wait_ge(*ready)
                pe.matmul(dst[:, at:at + SEQ], ones[:], src[:], start=True, stop=True).then_inc(stat_mm, 1)

            pe.wait_ge(consts, 9)
            pe.wait_ge(c_act, 1)
            stats((stat_in, 1), acc)
            pe.wait_ge(small_in, 48)
            pe.matmul(banks[0][0:HEADS, 0:384], rbx[:], bkt[:], start=True, stop=True).then_inc(bias_mm, 1)
            for q in range(12):
                rows(q, q % 4, mod_landed(q))
                cols(q, q % 2)
            pe.wait_ge(bias_cp, 1)
            for v in range(2):
                unit_ready("pool", 0, v)
                for mi in range(4):
                    m = 4 * v + mi
                    pe.wait_ge(pool_in, m // 2 + 1)
                    if m >= 4:
                        pe.wait_ge(tile_read, m - 3)
                    for kk in range(2):
                        k = 2 * (m // 2) + kk
                        mm = product(out_bank("pool", m)[:, 0:SEQ], v % HL, 2 * mi + kk, pool_hi[:, k, :], pool_lo[:, k, :],
                                     kk == 0, kk == 1)
                mm.then_inc(pe_units, 1)
            for q in range(12, MOD_FIRST):
                rows(q, q % 4, mod_landed(q))
                cols(q, q % 2)

            def whole(name, i, j, r_hi, r_lo, n, ready=None):
                unit_ready(name, i, j)
                if name == "qkv":
                    pe.wait_ge(tile_read, T0[name] + 8 * i + j - 2)
                else:
                    pe.wait_ge(tile_read, 8 * i + (T0[name] + j - 3))
                dst = out_bank(name, 8 * i + j if name == "qkv" else j)
                for k in range(DC):
                    if j == 0 and ready is not None:
                        pe.wait_ge(ready[0], ready[1] + k + 1)
                    mm = product(dst[:, 0:n], (U0[name] + j) % HL, k, r_hi[:, k, 0:n], r_lo[:, k, 0:n], k == 0, k == DC - 1)
                mm.then_inc(pe_units, 1)

            def with_piece(i, j, base):
                if j % 4 == 2:
                    rows(2 * i + (MOD_FIRST + base + j // 4), j // 4, 16 * i + (landed_base(j // 4) + 16 + 16 * (base // 2)))
                if j % 4 == 3:
                    cols(2 * i + (MOD_FIRST + base + j // 4), j // 4)

            def landed_base(s):
                return 16 * sum(mod_slot(q) == s for q in range(MOD_FIRST))

            def down(name, i, j):
                unit_ready(name, i, j)
                base = 0 if name == "down0" else 32
                dst = out_bank(name, j // 4)
                if j % 4 == 0:
                    pe.wait_ge(tile_read, 2 * i + (T0[name] + j // 4 - 1))
                for s in range(UT):
                    k = 8 * (j % 4) + s
                    if j < 4:
                        pe.wait_ge(hid_lo_done, base + k + 1)
                    mm = product(dst[:, 0:SEQ], (U0[name] + j) % HL, s, hid_hi[:, k, :], hid_lo[:, k, :], k == 0, k == FFC - 1)
                mm.then_inc(pe_units, 1)
                if name == "down0":
                    with_piece(i, j, 8)

            def first_down(name):
                pe.wait_ge(tile_read, T0[name])
                loop_units(pe, name, lambda i, j: down(name, i, j))

            def up_phase(name):
                pe.wait_ge(tile_read, T0[name])
                sums = (acc_done, 8 if name == "up0" else 26)
                pe.wait_ge(shift_done, 1 if name == "up0" else 3)

                def step(i, j):
                    whole(name, i, j, xg_hi, xg_lo, SEQ + 2, (xg_lo_done, 0 if name == "up0" else 16))
                    if name == "up0":
                        with_piece(i, j, 0)
                for j in range(8):
                    step(0, j)
                    if j == 0:
                        stats(sums, acc)
                with pe.Fori(1, 4) as i:
                    for j in range(8):
                        step(i, j)

            up_phase("up0")
            first_down("down0")

            def scores(a, e):
                pe.wait_ge(qkv_done, 3 * a + 2)
                if 2 * a + e:
                    pe.wait_ge(logit_done, 2 * a + e)
                else:
                    pe.wait_ge(var_done, 3)
                r = slice(64 * e, 64 * e + 64)
                pe.matmul(s_bank[:, 0:128], qT[r, a % 2, 0:128], kT[r, a % 2, 0:128], start=True, stop=True)
                pe.matmul(s_bank[:, 128:384], qT[r, a % 2, 128:256], kT[r, a % 2, :], start=True, stop=True)\
                    .then_inc(score_done, 1)

            def values(a):
                pe.wait_ge(qkv_done, 3 * a + 3)
                if a:
                    pe.wait_ge(pt_copied, 2 * a)
                pe.transpose(t_bank[:, 0:128], vT[:, a % 2, 0:128], ident[:])
                pe.transpose(t_bank[:, 128:256], vT[:, a % 2, 128:256], ident[:]).then_inc(vt_done, 1)

            def turn(a, e):
                pe.wait_ge(prob_done, 2 * a + e + 1)
                if e == 0:
                    pe.wait_ge(vt_copied, a + 1)
                else:
                    pe.wait_ge(pt_copied, 2 * a + 1)
                for b in range(3):
                    mm = pe.transpose(t_bank[:, b * P:(b + 1) * P], probn[:, e, b * P:(b + 1) * P], ident[:])
                mm.then_inc(pt_done, 1)

            def weigh(a):
                pe.wait_ge(pt_copied, 2 * a + 2)
                if a:
                    pe.wait_ge(o_lo_done, a)
                for e in range(2):
                    dst = o_bank[64 * e:64 * e + 64, :]
                    pe.matmul(dst[:, 0:256], vtok[:, a % 2, 64 * e:64 * e + 64], pT[:, e, 0:256], start=True, stop=False,
                              skip_group_check=True)
                    mm = pe.matmul(dst[:, 128:256], vtok[:, a % 2, 128 + 64 * e:192 + 64 * e], pT[:, e, 256:384],
                                   start=False, stop=True, skip_group_check=True)
                mm.then_inc(pv_done, 1)

            pe.wait_ge(tile_read, T0["qkv"])
            pe.wait_ge(shift_done, 2)
            for j in range(DC + 2):
                a = j - 1
                for part in range(3):
                    v = 3 * j + part
                    if j < DC:
                        whole("qkv", v // 8, v % 8, xg_hi, xg_lo, SEQ + 2, (xg_lo_done, 8))
                    if v == 0:
                        stats((acc_done, 17), acc)
                    if part == 0:
                        if 0 <= a < DC:
                            scores(a, 0)
                        if 1 <= a <= DC:
                            turn(a - 1, 1)
                        if j < DC:
                            rows(36 + j, j % 2, mod_landed(36 + j))
                    if part == 1:
                        if 0 <= a < DC:
                            scores(a, 1)
                        if 1 <= a <= DC:
                            weigh(a - 1)
                        if 0 <= a < DC:
                            values(a)
                        if j < DC:
                            cols(36 + j, j % 2)
                    if part == 2 and 0 <= a < DC:
                        turn(a, 0)

            pe.wait_ge(tile_read, T0["o"])
            for j in range(8):
                whole("o", 0, j, o_hi, o_lo, SEQ, (o_lo_done, 0))
                if j % 2 == 0:
                    rows(44 + j // 2, (j // 2) % 2, mod_landed(44 + j // 2))
                else:
                    cols(44 + j // 2, (j // 2) % 2)
            up_phase("up1")
            first_down("down1")

            pe.wait_ge(tile_read, T0["rx"])
            for v in range(10):
                whole("rx", v // 8, v % 8, xg_hi, xg_lo, SEQ, (xg_lo_done, 24))
                if v == 0:
                    stats((acc_done, 35), acc)
                    stats((acc2_done, 9), acc2, SEQ)
            loop_units(pe, "glu", lambda i, j: whole("glu", i, j, xg_hi, xg_lo, SEQ))
            loop_units(pe, "rg", lambda i, j: whole("rg", i, j, xg_hi, xg_lo, SEQ))
            pe.wait_ge(tile_read, T0["gates"])
            g = 0
            for n, (m, which, k, start, stop) in enumerate(GATES):
                w, s = GATE_AT[n]
                if s == 0:
                    unit_ready("gates", 0, w)
                if start:
                    pe.wait_ge(act_lo_done, max(gate_tiles()[m]) + 1)
                    if g >= 4:
                        pe.wait_ge(gate_read, g - 3)
                mm = product(out_bank("gates", g)[:, 0:SEQ], (U0["gates"] + w) % HL, s, act_hi[:, k, :], act_lo[:, k, :],
                             start, stop)
                g += stop
                if n == len(GATES) - 1 or GATE_AT[n + 1][1] == 0:
                    mm.then_inc(pe_units, 1)
            pe.wait_ge(gate_read, 20)
            loop_units(pe, "gb", lambda i, j: whole("gb", i, j, xg_hi, xg_lo, SEQ))
            loop_units(pe, "ga", lambda i, j: whole("ga", i, j, xg_hi, xg_lo, SEQ))

            def halves(name, v, per, r_hi, r_lo, ready):
                h, r = v // per, v % per
                unit_ready(name, v // 8, v % 8)
                for s in range(UT):
                    k, m = 2 * r + s // 4, 4 * h + s % 4
                    if h == 0 and s % 4 == 0:
                        pe.wait_ge(ready[0], ready[1] + k + 1)
                    if r == 0 and s < 4:
                        pe.wait_ge(tile_read, T0[name] + (0 if name == "w2" else m - 3))
                    mm = product(out_bank(name, m)[:, 0:SEQ], (U0[name] + v) % HL, s, r_hi[:, k, :], r_lo[:, k, :],
                                 k == 0, k == 2 * per - 1)
                mm.then_inc(pe_units, 1)

            for v in range(10):
                halves("lru", v, 5, act_hi, act_lo, (act_lo_done, RC))
                if v == 2:
                    stats((stat_in, 2), acc2)
                if v == 6:
                    stats((stat_in, 3), acc2)
            for j in range(8):
                whole("conv", 0, j, xg_hi, xg_lo, SEQ, (ln_lo, 0))
            for j in range(8):
                whole("mix", 0, j, act_hi, act_lo, SEQ, (act_lo_done, 2 * RC))
            for j in range(8):
                whole("ffn", 0, j, xg_hi, xg_lo, SEQ, (xg_lo_done, 32))
                if j == 0:
                    stats((acc_done, 44), acc)
            with pe.Fori(1, 5) as i:
                for j in range(8):
                    whole("ffn", i, j, xg_hi, xg_lo, SEQ)
            for j in range(4):
                whole("ffn", 5, j, xg_hi, xg_lo, SEQ)
            for v in range(22):
                halves("w2", v, 11, f_hi, f_lo, (f_lo_done, 0))
            stats((acc_done, 53), acc, dst=banks[0])

        @block.scalar
        def _(act):
            def split(name, i, j):
                at = U0[name] + j + LEAD
                if isinstance(i, int) and 8 * i + at >= N_UNITS:
                    return
                slot = (at // 2) % RAW
                act.wait_ge(landed[slot], 16 * i + 16 * (at // 8 + 1))
                if not isinstance(i, int) or 8 * i + at >= HL:
                    act.wait_ge(pe_units, 8 * i + at - HL + 1)
                act.activation(w_hi[:, at % HL, :], raw[:, slot, (at % 2) * UT * P:(at % 2 + 1) * UT * P],
                               ACT.Copy).then_inc(hi_done, 1)

            def mod_copy(q, s):
                act.wait_ge(mod_rows, q + 1)
                if not isinstance(q, int) or q >= 2:
                    act.wait_ge(mod_cols, q - 1)
                act.activation(mod_row[:, s, :], row_bank[:, 0:SEQ], ACT.Copy).then_inc(mod_copied, 1)

            def mod_piece(i, j, base):
                if j % 4 == 2:
                    mod_copy(2 * i + (MOD_FIRST + base + j // 4), j // 4)

            def root(n):
                act.wait_ge(var_done, n)
                act.activation(newt[:, 0, :], var[:], ACT.Sqrt).then_inc(root_done, 1)

            act.wait_ge(x_in_s, 16)
            act.activation(h_pad[:, :, 16:], x[:], ACT.Square).then_inc(x_sq, 1)
            act.wait_ge(vec_in, 16)
            act.wait_ge(consts, 1)
            act.activation(cz[:, :, 0:1], vec[:, VEC["c"]:VEC["c"] + DC].rearrange("p (c a) -> p c a", a=1),
                           ACT.Silu).then_inc(c_act, 1)
            act.activation(sp[:, 0, :], col("lam", 0, RC), ACT.Abs).then_inc(c_act, 1)
            act.wait_ge(c_act, 2)
            act.activation(sp[:, 1, :], sp[:, 0, :], ACT.Exp, scale=-1.0).then_inc(c_act, 1)
            root(1)
            for q in range(8):
                mod_copy(q, q % 2)
            act.wait_ge(xr_done, 1)
            act.wait_ge(gain_done, 1)
            act.wait_ge(mod_read, 2)
            for m in range(DC):
                act.activation(h_pad[:, m, 16:], h_pad[:, m, 16:], ACT.Identity, bias=modv[:, 8 * SH1 + m:8 * SH1 + m + 1],
                               scale=gain[:, 0, m:m + 1]).then_inc(h_done, 1)
            for q in range(8, 12):
                mod_copy(q, q % 2)
            for v in (-3, -2):
                split("pool", 0, v)

            def res_square(name, n, i, j, gains, m_end=None):
                m = 2 * i + j
                act.wait_ge(tile_read, 2 * i + (T0[name] + j + 1))
                if name == "down1":
                    act.activation(sq[:, 0, :], chunk(x, m), ACT.Square)
                    act.activation(sq[:, 1, :], chunk(x, m), ACT.Square, scale=col_at("norm_final", m)).then_inc(sq_done, 1)
                else:
                    act.activation(sq[:, j % 2, :], chunk(x, m), ACT.Square).then_inc(sq_done, 1)
                if gains is not None:
                    act.activation(chunk(xg_hi, m), chunk(x, m), ACT.Copy, scale=gains(m)).then_inc(xg_hi_done, 1)

            def col_at(name, m):
                return vec[:, bass.ds(m + VEC[name], 1)] if not isinstance(m, int) else col(name, m)

            def gain_at(n):
                return lambda m: gain[:, n, one(m)]

            for m in range(DC):
                act.wait_ge(tile_read, m + 1)
                if m >= 2:
                    act.wait_ge(acc_done, m)
                act.activation(sq[:, m % 2, :], x[:, m, :], ACT.Square).then_inc(sq_done, 1)
            for q in range(12, MOD_FIRST):
                mod_copy(q, q % 2)
                if q == 16:
                    act.wait_ge(gain_done, 2)
                    for m in range(DC):
                        act.activation(xg_hi[:, m, 0:SEQ], x[:, m, :], ACT.Copy, scale=gain[:, 1, m:m + 1]).then_inc(xg_hi_done, 1)
            for v in (-1, 0, 1):
                split("pool", 0, v)

            def up(name, i, j):
                split(name, i, j)
                act.wait_ge(tile_read, 8 * i + (T0[name] + j + 1))
                base = 0 if name == "up0" else 32
                act.activation(ub[:, j % 2, :], ab[:, j % 2, 0:SEQ], ACT.Relu, bias=ab[:, j % 2, SEQ:SEQ + 1]).then_inc(relu_done, 1)
                act.wait_ge(relu_done, 8 * i + (base + j + 1))
                act.activation(sb2[:, j % 2, :], ub[:, j % 2, :], ACT.Square).then_inc(sq2_done, 1)
                if name == "up0":
                    mod_piece(i, j, 0)

            def up_phase(name, n):
                for j in range(8):
                    if j == 0:
                        split(name, 0, j)
                        root(n)
                        act.wait_ge(tile_read, T0[name] + 1)
                        base = 0 if name == "up0" else 32
                        act.activation(ub[:, 0, :], ab[:, 0, 0:SEQ], ACT.Relu, bias=ab[:, 0, SEQ:SEQ + 1]).then_inc(relu_done, 1)
                        act.wait_ge(relu_done, base + 1)
                        act.activation(sb2[:, 0, :], ub[:, 0, :], ACT.Square).then_inc(sq2_done, 1)
                    else:
                        up(name, 0, j)
                act.preload_act_table(ACT.Relu)
                with act.Fori(1, 4) as i:
                    for j in range(8):
                        up(name, i, j)

            def down(name, i, j, n, gains):
                split(name, i, j)
                if j % 4 == 3:
                    res_square(name, n, i, j // 4, gains)
                if name == "down0":
                    mod_piece(i, j, 8)

            up_phase("up0", 2)
            act.wait_ge(gain_done, 3)
            loop_units(act, "down0", lambda i, j: down("down0", i, j, 1, gain_at(2)))

            def exps(a, e):
                act.wait_ge(neg_done, 2 * a + e + 1)
                act.activation(prob[:, e, 0:128], logit[:, e, 0:128], ACT.Exp, bias=smx[:, e, 2:3], accum_out=smx[:, e, 4:5])
                act.activation(prob[:, e, 128:384], logit[:, e, 128:384], ACT.Exp, bias=smx[:, e, 3:4],
                               accum_out=smx[:, e, 5:6]).then_inc(exp_done, 1)

            def copy_pt(a, e):
                act.wait_ge(pt_done, 2 * a + e + 1)
                if a:
                    act.wait_ge(pv_done, a)
                act.activation(pT[:, e, :], t_bank[:, 0:384], ACT.Copy).then_inc(pt_copied, 1)

            for j in range(DC + 2):
                a = j - 1
                for part in range(3):
                    v = 3 * j + part
                    if j < DC:
                        split("qkv", v // 8, v % 8)
                        if v == 0:
                            root(3)
                        act.wait_ge(tile_read, T0["qkv"] + v + 1)
                        if j >= 2:
                            if part < 2:
                                act.wait_ge(score_done, 2 * (j - 2) + 2)
                            else:
                                act.wait_ge(vt_done, j - 1)
                        act.activation(reverse(qT[:, j % 2, :]) if part == 0 else (kT, vT)[part - 1][:, j % 2, :],
                                       ab[:, v % 2, 0:SEQ].rearrange("p (b n) -> p b n", b=2) if part == 0 else ab[:, v % 2, 0:SEQ], ACT.Identity,
                                       bias=ab[:, v % 2, SEQ:SEQ + 1]).then_inc(qkv_done, 1)
                    if part == 0:
                        if j < DC:
                            mod_copy(36 + j, j % 2)
                        if 1 <= a <= DC:
                            copy_pt(a - 1, 1)
                        if 0 <= a < DC:
                            exps(a, 0)
                    if part == 1 and 0 <= a < DC:
                        exps(a, 1)
                    if part == 2:
                        if 1 <= a <= DC:
                            act.wait_ge(pv_done, a)
                            act.activation(o_hi[:, a - 1, :].rearrange("p (b n) -> p b n", b=2), reverse(o_bank[:, 0:SEQ]), ACT.Copy).then_inc(o_hi_done, 1)
                        if 0 <= a < DC:
                            copy_pt(a, 0)

            act.wait_ge(gain_done, 4)
            for j in range(8):
                split("o", 0, j)
                if j % 2 == 0:
                    mod_copy(44 + j // 2, (j // 2) % 2)
                res_square("o", 2, 0, j, gain_at(3))
            up_phase("up1", 4)
            loop_units(act, "down1", lambda i, j: down("down1", i, j, 3, lambda m: gain1[:, one(m)]))

            def activate(name, n, k, dst, func, b):
                act.wait_ge(tile_read, T0[name] + n + 1)
                act.activation(dst, ab[:, n % 2, 0:SEQ], func, bias=col("b_in", b)).then_inc(z_done, 1)

            def xb_high(m):
                act.wait_ge(xb_done, m + 1)
                act.activation(act_hi[:, m, :], rx[:, m, RTAPS - 1:], ACT.Copy).then_inc(act_hi_done, 1)

            for v in range(10):
                split("rx", v // 8, v % 8)
                if v == 0:
                    root(5)
                    root(6)
                    act.wait_ge(pads, 1)
                activate("rx", v, v, rx[:, v, RTAPS - 1:], ACT.Identity, v)
                if v >= 1:
                    xb_high(v - 1)
            for v in range(16):
                split("glu", v // 8, v % 8)
                if v == 0:
                    xb_high(9)
                if v % 2 == 1:
                    m = v // 2
                    act.wait_ge(tile_read, T0["glu"] + v + 1)
                    if m >= 2:
                        act.wait_ge(u_done, m - 1)
                    act.activation(sq[:, m % 2, :], ab[:, 1, 0:SEQ], ACT.Sigmoid, bias=col("b_in", RC + v)).then_inc(z_done, 1)
            for v in range(10):
                split("rg", v // 8, v % 8)
                activate("rg", v, 0, grg[:, v, :], ACT.Gelu_apprx_tanh, 26 + v)
            g = 0
            for v in range(GATE_UNITS):
                split("gates", 0, v)
                while g < 20 and GATE_DONE[g] == v:
                    m, which = g // 2, g % 2
                    act.wait_ge(pe_units, U0["gates"] + v + 1)
                    act.activation((rt, ig)[which][:, m, :], out_bank("gates", g)[:, 0:SEQ], ACT.Sigmoid,
                                   bias=col(("ba", "bx")[which], m)).then_inc(gate_read, 1)
                    g += 1
            act.wait_ge(gate_read, 20)
            for m in range(RC):
                act.activation(av[:, m, :], rt[:, m, :], ACT.Exp, scale=sp[:, 6, m:m + 1]).then_inc(decay_done, 1)
            act.wait_ge(decay_done, RC)
            for m in range(RC):
                act.activation(rt[:, m, :], rt[:, m, :], ACT.Tanh, scale=sp[:, 7, m:m + 1]).then_inc(decay_done, 1)
            for v in range(8):
                split("gb", 0, v)
                activate("gb", v, 0, sgb[:, v, :], ACT.Sigmoid, 44 + v)
                if v == 5:
                    act.wait_ge(mult2_done, RC)
                    act.activation(rt[:], rt[:], ACT.Sqrt).then_inc(mult_done, 1)
            def hb_high(m):
                act.wait_ge(hb_done, m + 1)
                act.activation(act_hi[:, m, :], rt[:, m, :], ACT.Copy).then_inc(act_hi_done, 1)

            for v in range(8):
                split("ga", 0, v)
                activate("ga", v, 0, sga[:, v, :], ACT.Sigmoid, 36 + v)
                hb_high(v)
            hb_high(8)
            hb_high(9)
            for v in range(10):
                split("lru", v // 8, v % 8)
                if v == 2:
                    act.wait_ge(ln_c, 1)
                    act.activation(u[:, :, 0:SEQ], y[:], ACT.Square).then_inc(ln_sq, 1)
                if v == 6:
                    root(7)
            act.wait_ge(ln_n, 1)
            for m in range(DC):
                act.activation(y[:, m, :], y[:, m, :], ACT.Silu, bias=col("ln_b", m), scale=col("ln_g", m)).then_inc(ln_silu, 1)
                act.wait_ge(ln_silu, m + 1)
                act.activation(xg_hi[:, m, 0:SEQ], y[:, m, :], ACT.Copy).then_inc(ln_hi, 1)
            for m in range(8):
                split("conv", 0, m)
                act.wait_ge(m_done, m + 1)
                act.activation(act_hi[:, m, :], sga[:, m, :], ACT.Copy).then_inc(act_hi_done, 1)
            for m in range(8):
                split("mix", 0, m)
                res_square("mix", 4, 0, m, lambda m: col("norm2", m))

            def ffn(i, j):
                split("ffn", i, j)
                if j % 2 == 0:
                    act.wait_ge(tile_read, 8 * i + (T0["ffn"] + j + 1))
                    act.activation(sq[:, (j // 2) % 2, :], ab[:, 0, 0:SEQ], ACT.Silu).then_inc(f_silu, 1)

            for j in range(8):
                if j == 0:
                    split("ffn", 0, 0)
                    root(8)
                    act.wait_ge(tile_read, T0["ffn"] + 1)
                    act.activation(sq[:, 0, :], ab[:, 0, 0:SEQ], ACT.Silu).then_inc(f_silu, 1)
                else:
                    ffn(0, j)
            act.preload_act_table(ACT.Silu)
            with act.Fori(1, 5) as i:
                for j in range(8):
                    ffn(i, j)
            for j in range(4):
                ffn(5, j)
            for v in range(22):
                split("w2", v // 8, v % 8)
                if v in (11, 21):
                    for m in range(4 * (v // 21), 4 * (v // 21) + 4):
                        res_square("w2", 5, 0, m, None)
            root(9)

        @block.vector
        def _(ve):
            chain = [0]

            def link(ins):
                chain[0] += 1
                ins.then_inc(dve, 1)
                ve.wait_ge(dve, chain[0])

            def split(name, i, j):
                at = U0[name] + j + LEAD
                if isinstance(i, int) and 8 * i + at >= N_UNITS:
                    return
                slot = (at // 2) % RAW
                ve.wait_ge(hi_done, 8 * i + at + 1)
                ve.tensor_tensor(w_lo[:, at % HL, :], raw[:, slot, (at % 2) * UT * P:(at % 2 + 1) * UT * P],
                                 w_hi[:, at % HL, :].bitcast(F32), ALU.subtract).then_inc(lo_done, 1)

            def rsqrt(n, dst, first=True):
                ve.wait_ge(root_done, n)
                link(ve.reciprocal(newt[:, 1, :], newt[:, 0, :]))
                link(ve.tensor_tensor(newt[:, 0, :], newt[:, 1, :], newt[:, 1, :], ALU.mult))
                link(ve.tensor_tensor(newt[:, 0, :], newt[:, 0, :], var[:], ALU.mult))
                link(ve.tensor_scalar(newt[:, 0, :], newt[:, 0, :], -0.5, 1.5, ALU.mult, ALU.add))
                link(ve.tensor_tensor(dst, newt[:, 1, :], newt[:, 0, :], ALU.mult))

            def variance(n, nv, src):
                ve.wait_ge(stat_mm, n)
                ve.tensor_scalar(var[:], src[:, 0:SEQ], 1.0 / D, EPS, ALU.mult, ALU.add).then_inc(var_done, 1)

            def norm(n, nv, dst, src=stat_bank):
                variance(n, nv, src)
                rsqrt(nv, dst)

            def over_chunks(t):
                return t.rearrange("p c t -> p t c")

            def mod_group(g):
                ve.wait_ge(mod_cols, 4 * g + 4)
                ve.tensor_tensor(modv[:, 8 * g:8 * g + 8], col_banks[g % 2][:, 0:8], col("b_mod", 8 * g, 8), ALU.add).then_inc(mod_read, 1)
                ve.wait_ge(mod_read, g + 1)

            def mod_two(q, wait=True):
                ve.wait_ge(mod_cols, q + 1)
                c = 2 * q
                ve.tensor_tensor(modv[:, bass.ds(c, 2)], col_banks[0][:, 0:2], vec[:, bass.ds(c + VEC["b_mod"], 2)], ALU.add).then_inc(mod_read, 1)

            def mod_two_at(i, j, base):
                if j % 4 == 3:
                    mod_two(2 * i + (MOD_FIRST + base + j // 4))

            def make_gain(n, sc, norm_col):
                ve.scalar_tensor_tensor(gain[:, n, :], modv[:, sc:sc + DC], 1.0, norm_col, ALU.add, ALU.mult).then_inc(gain_done, 1)

            def shift(at):
                src = modv[:, at:at + DC].rearrange("p (c a) -> p c a", a=1).broadcast_to((P, DC, 2))
                link(ve.tensor_copy(xg_hi[:, :, SEQ:SEQ + 2], src))
                ve.tensor_tensor(xg_lo[:, :, SEQ:SEQ + 2], src, xg_hi[:, :, SEQ:SEQ + 2].bitcast(F32), ALU.subtract).then_inc(shift_done, 1)

            ve.wait_ge(x_sq, 1)
            ve.tensor_reduce(acc[:], over_chunks(h_pad[:, :, 16:]), AX.X, ALU.add).then_inc(stat_in, 1)
            ve.wait_ge(vec_in, 16)
            ve.wait_ge(c_act, 3)
            link(ve.tensor_scalar(sp[:, 2, :], sp[:, 1, :], 2.0, None, ALU.add))
            link(ve.reciprocal(sp[:, 3, :], sp[:, 2, :]))
            link(ve.tensor_tensor(sp[:, 2, :], sp[:, 1, :], sp[:, 3, :], ALU.mult))
            link(ve.tensor_tensor(sp[:, 3, :], sp[:, 2, :], sp[:, 2, :], ALU.mult))
            link(ve.tensor_scalar(sp[:, 4, :], sp[:, 3, :], 1.0 / 17, 1.0 / 15, ALU.mult, ALU.add))
            for k in (13, 11, 9, 7, 5, 3, 1):
                link(ve.tensor_tensor(sp[:, 4, :], sp[:, 4, :], sp[:, 3, :], ALU.mult))
                link(ve.tensor_scalar(sp[:, 4, :], sp[:, 4, :], 1.0 / k, None, ALU.add))
            link(ve.scalar_tensor_tensor(sp[:, 5, :], sp[:, 4, :], 2.0, sp[:, 2, :], ALU.mult, ALU.mult))
            link(ve.tensor_scalar(sp[:, 4, :], col("lam", 0, RC), -1.0, 0.0, ALU.mult, ALU.max))
            link(ve.tensor_tensor(sp[:, 5, :], sp[:, 5, :], sp[:, 4, :], ALU.add))
            link(ve.tensor_scalar(sp[:, 6, :], sp[:, 5, :], -8.0, None, ALU.mult))
            link(ve.tensor_scalar(sp[:, 7, :], sp[:, 5, :], 8.0, None, ALU.mult))
            link(ve.tensor_tensor(gain1[:], col("norm_final", 0, DC), col("norm1", 0, DC), ALU.mult))
            norm(1, 1, rstd[:, 0:SEQ])
            ve.tensor_tensor(h_pad[:, :, 16:], x[:], rstd[:, 0:SEQ].rearrange("p (a n) -> p a n", a=1).broadcast_to((P, DC, SEQ)),
                             ALU.mult).then_inc(xr_done, 1)
            ve.wait_ge(bias_mm, 1)
            ve.tensor_copy(bydist[:], banks[0][0:HEADS, 0:384]).then_inc(bias_cp, 1)
            mod_group(0)
            make_gain(0, 8 * SC1, col("norm_mix", 0, DC))
            mod_group(1)

            ve.wait_ge(h_done, DC)
            ve.wait_ge(consts, 9)
            ve.wait_ge(inv_in, 16)
            W = slice(16, 16 + SEQ)
            link(ve.tensor_tensor(s2[:, :, W], h_pad[:, :, W], h_pad[:, :, 15:15 + SEQ], ALU.add))
            link(ve.tensor_tensor(s4[:, :, W], s2[:, 2:8, W], s2[:, 2:8, 14:14 + SEQ], ALU.add))
            link(ve.tensor_tensor(s8[:, :, W], s4[:, 2:6, W], s4[:, 2:6, 12:12 + SEQ], ALU.add))
            link(ve.tensor_tensor(s16[:, :, W], s8[:, 2:4, W], s8[:, 2:4, 8:8 + SEQ], ALU.add))
            for g, t in enumerate((s2, s4, s8, s16)):
                part = t[:, 0:2, W]
                link(ve.tensor_tensor(part, part, invc[:, g:g + 1, :].broadcast_to((P, 2, SEQ)), ALU.mult))
                link(ve.tensor_tensor(part, part, h_pad[:, 2 * g:2 * g + 2, W], ALU.subtract))
                link(ve.tensor_copy(pool_hi[:, 2 * g:2 * g + 2, :], part))
                ve.tensor_tensor(pool_lo[:, 2 * g:2 * g + 2, :], part, pool_hi[:, 2 * g:2 * g + 2, :].bitcast(F32),
                                 ALU.subtract).then_inc(pool_in, 1)
            mod_group(2)
            link(ve.tensor_tensor(gate0[:], modv[:, 8 * G1:8 * G1 + DC], col("pool_scale", 0, DC), ALU.mult))
            for v in (-3, -2):
                split("pool", 0, v)
            for m in range(DC):
                if m % 4 == 0:
                    ve.wait_ge(pe_units, m // 4 + 1)
                ve.scalar_tensor_tensor(x[:, m, :], out_bank("pool", m)[:, 0:SEQ], gate0[:, m:m + 1], x[:, m, :], ALU.mult,
                                        ALU.add).then_inc(tile_read, 1)
            for m in range(DC):
                ve.wait_ge(sq_done, m + 1)
                if m:
                    ve.wait_ge(acc_done, m)
                    ve.tensor_tensor(acc[:], acc[:], sq[:, m % 2, :], ALU.add).then_inc(acc_done, 1)
                else:
                    ve.tensor_copy(acc[:], sq[:, 0, :]).then_inc(acc_done, 1)
            mod_group(3)
            make_gain(1, 8 * SC2, col("norm_mlp", 0, DC))
            ve.wait_ge(gain_done, 2)
            for m in range(DC):
                ve.wait_ge(xg_hi_done, m + 1)
                ve.scalar_tensor_tensor(xg_lo[:, m, 0:SEQ], x[:, m, :], gain[:, 1, m:m + 1], xg_hi[:, m, 0:SEQ].bitcast(F32),
                                        ALU.mult, ALU.subtract).then_inc(xg_lo_done, 1)
            mod_group(4)
            shift(8 * SH2)
            for v in (-1, 0, 1):
                split("pool", 0, v)

            def up(name, i, j, ahead=True):
                if ahead:
                    split(name, i, j)
                base = 0 if name == "up0" else 32
                ve.wait_ge(pe_units, 8 * i + (U0[name] + j + 1))
                ve.tensor_tensor(ab[:, j % 2, :], out_bank(name, j)[:, 0:SEQ + 2], rstd[:], ALU.mult).then_inc(tile_read, 1)
                t = 8 * i + j
                ve.wait_ge(sq2_done, 8 * i + (base + j + 1))
                ve.tensor_copy(chunk(hid_hi, t), sb2[:, j % 2, :]).then_inc(hid_hi_done, 1)
                ve.wait_ge(hid_hi_done, 8 * i + (base + j + 1))
                ve.tensor_tensor(chunk(hid_lo, t), sb2[:, j % 2, :], chunk(hid_hi, t).bitcast(F32),
                                 ALU.subtract).then_inc(hid_lo_done, 1)
                if name == "up0":
                    mod_two_at(i, j, 0)

            def up_phase(name, n):
                split(name, 0, 0)
                norm(n, n, rstd[:, 0:SEQ])
                for j in range(8):
                    up(name, 0, j, ahead=j > 0)
                with ve.Fori(1, 4) as i:
                    for j in range(8):
                        up(name, i, j)

            def clear(n, two=False):
                ve.memset(acc[:], 0.0).then_inc(acc_done, 1)
                if two:
                    ve.memset(acc2[:], 0.0).then_inc(acc2_done, 1)

            def residual(name, i, j, gate):
                m = 2 * i + j
                dst, src = chunk(x, m), out_bank(name, j)[:, 0:SEQ]
                if gate is None:
                    ve.tensor_tensor(dst, src, dst, ALU.add).then_inc(tile_read, 1)
                else:
                    g = modv[:, gate + m:gate + m + 1] if isinstance(m, int) else modv[:, bass.ds(m + gate, 1)]
                    ve.scalar_tensor_tensor(dst, src, g, dst, ALU.mult, ALU.add).then_inc(tile_read, 1)

            def finish(name, n, i, j, gains):
                m = 2 * i + j
                ve.wait_ge(sq_done, 2 * i + (8 * n + j + 1))
                ve.wait_ge(acc_done, 2 * i + (9 * n + j))
                if name == "down1":
                    ve.wait_ge(acc2_done, 2 * i + (j + 1))
                    ve.tensor_tensor(acc2[:], acc2[:], sq[:, 1, :], ALU.add).then_inc(acc2_done, 1)
                ve.tensor_tensor(acc[:], acc[:], sq[:, 0 if name == "down1" else j % 2, :], ALU.add).then_inc(acc_done, 1)
                if gains is not None:
                    ve.wait_ge(xg_hi_done, 2 * i + (8 * n + j + 1))
                    src = xg_hi[:, one(m), 0:SEQ].rearrange("p a n -> p (a n)")
                    dst = xg_lo[:, one(m), 0:SEQ].rearrange("p a n -> p (a n)")
                    ve.scalar_tensor_tensor(dst, chunk(x, m), gains(m), src.bitcast(F32), ALU.mult, ALU.subtract)\
                        .then_inc(xg_lo_done, 1)

            def down(name, n, i, j, gate, gains):
                split(name, i, j)
                if j % 4 == 3:
                    ve.wait_ge(pe_units, 8 * i + (U0[name] + j + 1))
                    residual(name, i, j // 4, gate)
                    finish(name, n, i, j // 4, gains)
                if name == "down0":
                    mod_two_at(i, j, 8)

            up_phase("up0", 2)
            ve.wait_ge(mod_read, 13)
            make_gain(2, 48 + 8 * SC1, col("norm_mix", 8, DC))
            ve.wait_ge(gain_done, 3)
            clear(1)
            loop_units(ve, "down0", lambda i, j: down("down0", 1, i, j, 8 * G2, lambda m: gain[:, 2, one(m)]))
            ve.wait_ge(mod_read, 21)
            shift(48 + 8 * SH1)

            def logits(a, e):
                h = 2 * a + e
                ve.wait_ge(toep_in[a % 2], 32 * (a // 2 + 1))
                ve.wait_ge(score_done, h + 1)
                ve.scalar_tensor_tensor(logit[:, e, :], s_bank[:, 0:384], float(HD) ** -0.5, toep[:, a % 2, e, :],
                                        ALU.mult, ALU.add).then_inc(logit_done, 1)
                ve.wait_ge(logit_done, h + 1)
                ve.tensor_reduce(smx[:, e, 0:1], logit[:, e, 0:128], AX.X, ALU.max)
                ve.tensor_reduce(smx[:, e, 1:2], logit[:, e, 128:384], AX.X, ALU.max).then_inc(max_done, 1)
                ve.wait_ge(max_done, h + 1)
                ve.tensor_scalar(smx[:, e, 2:4], smx[:, e, 0:2], -1.0, None, ALU.mult).then_inc(neg_done, 1)

            def normalize(a, e):
                ve.wait_ge(exp_done, 2 * a + e + 1)
                link(ve.reciprocal(smx[:, e, 6:8], smx[:, e, 4:6]))
                ve.tensor_scalar(probn[:, e, 0:128], prob[:, e, 0:128], smx[:, e, 6:7], None, ALU.mult)
                ve.tensor_scalar(probn[:, e, 128:384], prob[:, e, 128:384], smx[:, e, 7:8], None, ALU.mult).then_inc(prob_done, 1)

            for j in range(DC + 2):
                a = j - 1
                for part in range(3):
                    v = 3 * j + part
                    if j < DC:
                        split("qkv", v // 8, v % 8)
                        if v == 0:
                            norm(3, 3, rstd[:, 0:SEQ])
                        ve.wait_ge(pe_units, U0["qkv"] + v + 1)
                        if v >= 2:
                            ve.wait_ge(qkv_done, v - 1)
                        ve.tensor_tensor(ab[:, v % 2, :], out_bank("qkv", v)[:, 0:SEQ + 2], rstd[:], ALU.mult).then_inc(tile_read, 1)
                    if part == 0 and 0 <= a < DC:
                        logits(a, 0)
                    if part == 1:
                        if 0 <= a < DC:
                            normalize(a, 0)
                            logits(a, 1)
                        if j < DC:
                            mod_two(36 + j)
                    if part == 2:
                        if 0 <= a < DC:
                            ve.wait_ge(vt_done, a + 1)
                            ve.tensor_copy(vtok[:, a % 2, :], t_bank[:, 0:256]).then_inc(vt_copied, 1)
                            normalize(a, 1)
                        if 1 <= a <= DC:
                            ve.wait_ge(o_hi_done, a)
                            two = [t[:, a - 1, :].rearrange("p (b n) -> p b n", b=2) for t in (o_lo, o_hi)]
                            ve.tensor_tensor(two[0], reverse(o_bank[:, 0:SEQ]), two[1].bitcast(F32), ALU.subtract).then_inc(o_lo_done, 1)

            ve.wait_ge(mod_read, 29)
            make_gain(3, 48 + 8 * SC2, col("norm_mlp", 8, DC))
            ve.wait_ge(gain_done, 4)
            shift(48 + 8 * SH2)
            clear(2)
            for j in range(8):
                split("o", 0, j)
                ve.wait_ge(pe_units, U0["o"] + j + 1)
                residual("o", 0, j, 48 + 8 * G1)
                finish("o", 2, 0, j, lambda m: gain[:, 3, one(m)])
                if j % 2 == 1:
                    mod_two(44 + j // 2)
            up_phase("up1", 4)
            ve.wait_ge(mod_read, 33)
            clear(3, two=True)
            loop_units(ve, "down1", lambda i, j: down("down1", 3, i, j, 48 + 8 * G2, lambda m: gain1[:, one(m)]))

            def scaled(name, v, w=SEQ):
                ve.wait_ge(pe_units, U0[name] + v + 1)
                ve.tensor_tensor(ab[:, v % 2, 0:SEQ], out_bank(name, v)[:, 0:SEQ], rstd[:, 0:SEQ], ALU.mult).then_inc(tile_read, 1)

            def recurrent_conv(m):
                ve.wait_ge(z_done, m + 1)
                ve.wait_ge(pads, 1)
                t = newt[:, m % 2, :]
                link(ve.tensor_scalar(t, rx[:, m, 0:SEQ], col("rw", m), col("rb", m), ALU.mult, ALU.add))
                for k in (1, 2):
                    link(ve.scalar_tensor_tensor(t, rx[:, m, k:k + SEQ], col("rw", RC * k + m), t, ALU.mult, ALU.add))
                ve.scalar_tensor_tensor(rx[:, m, 3:3 + SEQ], rx[:, m, 3:3 + SEQ], col("rw", RC * 3 + m), t, ALU.mult, ALU.add)\
                    .then_inc(xb_done, 1)

            def low(n, m, src, ready):
                ve.wait_ge(*ready)
                ve.wait_ge(act_hi_done, n + 1)
                ve.tensor_tensor(act_lo[:, m, :], src, act_hi[:, m, :].bitcast(F32), ALU.subtract).then_inc(act_lo_done, 1)

            def xb_low(m):
                low(m, m, rx[:, m, 3:3 + SEQ], (xb_done, m + 1))

            def taps(n0, n1):
                for n in range(n0, min(n1, TAPS * DC)):
                    m, k = n // TAPS, n % TAPS
                    src = u[:, m, k:k + SEQ]
                    if k == 0:
                        ve.wait_ge(pads, 2)
                        ve.wait_ge(u_done, m + 1)
                        ve.tensor_scalar(y[:, m, :], src, col("dw_w", m), col("dw_b", m), ALU.mult, ALU.add).then_inc(tap_done, 1)
                    else:
                        ve.wait_ge(tap_done, n)
                        ve.scalar_tensor_tensor(y[:, m, :], src, col("dw_w", DC * k + m), y[:, m, :], ALU.mult, ALU.add)\
                            .then_inc(tap_done, 1)

            for v in range(10):
                split("rx", v // 8, v % 8)
                if v == 0:
                    norm(6, 5, rstd1[:])
                    link(ve.tensor_tensor(newt[:, 1, :], rstd1[:], rstd1[:], ALU.mult))
                    link(ve.scalar_tensor_tensor(newt[:, 1, :], stat_bank[:, SEQ:2 * SEQ], 1.0 / D, newt[:, 1, :], ALU.mult, ALU.mult))
                    ve.tensor_scalar(var[:], newt[:, 1, :], EPS, None, ALU.add).then_inc(var_done, 1)
                    rsqrt(6, rstd[:, 0:SEQ])
                    link(ve.tensor_tensor(rstd[:, 0:SEQ], rstd[:, 0:SEQ], rstd1[:], ALU.mult))
                if v >= 2:
                    ve.wait_ge(z_done, v - 1)
                scaled("rx", v)
                if v >= 1:
                    recurrent_conv(v - 1)
                if v >= 2:
                    xb_low(v - 2)
            for v in range(16):
                split("glu", v // 8, v % 8)
                m = v // 2
                if v == 0:
                    ve.wait_ge(z_done, 9)
                elif v % 2 == 0:
                    ve.wait_ge(u_done, m)
                else:
                    ve.wait_ge(z_done, 10 + m)
                scaled("glu", v)
                if v == 0:
                    recurrent_conv(9)
                    xb_low(8)
                if v == 1:
                    xb_low(9)
                    ve.wait_ge(pads, 2)
                if v < 8:
                    ve.scalar_tensor_tensor(x[:, v, :], x[:, v, :], col("norm_final", v), rstd1[:], ALU.mult, ALU.mult)
                if v % 2 == 1:
                    ve.wait_ge(z_done, 10 + m + 1)
                    ve.scalar_tensor_tensor(u[:, m, TAPS - 1:], ab[:, 0, 0:SEQ], col("b_in", RC + v - 1), sq[:, m % 2, :],
                                            ALU.add, ALU.mult).then_inc(u_done, 1)
                if v >= 2:
                    taps(5 * (v - 2), 5 * (v - 1))
            for v in range(10):
                split("rg", v // 8, v % 8)
                if v == 0:
                    ve.wait_ge(u_done, 8)
                else:
                    ve.wait_ge(z_done, 18 + v - 1)
                scaled("rg", v)
                taps(70 + 5 * v, 75 + 5 * v)
            for v in range(GATE_UNITS):
                split("gates", 0, v)
                taps(120 + 6 * v, 126 + 6 * v)

            def mult2(m):
                ve.wait_ge(decay_done, RC + m + 1)
                t = sq[:, m % 2, :]
                link(ve.tensor_tensor(t, av[:, m, :], av[:, m, :], ALU.mult))
                ve.scalar_tensor_tensor(rt[:, m, :], t, 1.0, rt[:, m, :], ALU.add, ALU.mult).then_inc(mult2_done, 1)

            def recurrence(m):
                ve.wait_ge(mult_done, 1)
                link(ve.tensor_tensor(ig[:, m, :], ig[:, m, :], rx[:, m, 3:3 + SEQ], ALU.mult))
                link(ve.tensor_tensor(ig[:, m, :], ig[:, m, :], rt[:, m, :], ALU.mult))
                link(ve.tensor_tensor_scan(rt[:, m, :], av[:, m, :], ig[:, m, :], 0.0, ALU.mult, ALU.add))
                ve.tensor_tensor(rt[:, m, :], rt[:, m, :], grg[:, m, :], ALU.mult).then_inc(hb_done, 1)

            def hb_low(m):
                low(RC + m, m, rt[:, m, :], (hb_done, m + 1))

            for v in range(8):
                split("gb", 0, v)
                ve.wait_ge(z_done, 28 + v - (1 if v else 0))
                scaled("gb", v)
                if v < 5:
                    mult2(2 * v)
                    mult2(2 * v + 1)
                taps(168 + 5 * v, 173 + 5 * v)
            for v in range(8):
                split("ga", 0, v)
                ve.wait_ge(z_done, 36 + v - (1 if v else 0))
                scaled("ga", v)
                recurrence(v)
                if v >= 1:
                    hb_low(v - 1)
                taps(208 + 5 * v, 213 + 5 * v)
            recurrence(8)
            recurrence(9)
            for m in (7, 8, 9):
                hb_low(m)

            def layernorm_steps(v):
                if v == 1:
                    ve.wait_ge(tap_done, TAPS * DC)
                    ve.tensor_reduce(acc2[:], over_chunks(y[:]), AX.X, ALU.add).then_inc(stat_in, 1)
                if v == 2:
                    ve.wait_ge(stat_mm, 7)
                    link(ve.tensor_scalar(newt[:, 0, :], stat_bank[:, 0:SEQ], 1.0 / D, None, ALU.mult))
                    ve.tensor_tensor(y[:], y[:], newt[:, 0:1, :].broadcast_to((P, DC, SEQ)), ALU.subtract).then_inc(ln_c, 1)
                if v == 4:
                    ve.wait_ge(ln_sq, 1)
                    ve.tensor_reduce(acc2[:], over_chunks(u[:, :, 0:SEQ]), AX.X, ALU.add).then_inc(stat_in, 1)
                if v == 6:
                    norm(8, 7, rstd1[:])
                    ve.tensor_tensor(y[:], y[:], rstd1[:].rearrange("p (a n) -> p a n", a=1).broadcast_to((P, DC, SEQ)),
                                     ALU.mult).then_inc(ln_n, 1)

            for v in range(10):
                split("lru", v // 8, v % 8)
                layernorm_steps(v)
                if v in (5, 9):
                    ve.wait_ge(pe_units, U0["lru"] + v + (v == 9))
                    for m in range(4 * (v == 9), 4 * (v == 9) + 4):
                        if m == 0:
                            ve.wait_ge(z_done, 44)
                        ve.tensor_tensor(sgb[:, m, :], out_bank("lru", m)[:, 0:SEQ], sgb[:, m, :], ALU.mult).then_inc(tile_read, 1)
            for m in range(DC):
                ve.wait_ge(ln_hi, m + 1)
                ve.tensor_tensor(xg_lo[:, m, 0:SEQ], y[:, m, :], xg_hi[:, m, 0:SEQ].bitcast(F32), ALU.subtract).then_inc(ln_lo, 1)
            for m in range(8):
                split("conv", 0, m)
                ve.wait_ge(pe_units, U0["conv"] + m + 1)
                ve.scalar_tensor_tensor(sga[:, m, :], out_bank("conv", m)[:, 0:SEQ], col("cb", m), sga[:, m, :], ALU.add,
                                        ALU.mult).then_inc(tile_read, 1)
                ve.wait_ge(tile_read, T0["conv"] + m + 1)
                ve.tensor_tensor(sga[:, m, :], sga[:, m, :], sgb[:, m, :], ALU.add).then_inc(m_done, 1)
                low(2 * RC + m, m, sga[:, m, :], (m_done, m + 1))
            clear(4)
            for m in range(8):
                split("mix", 0, m)
                ve.wait_ge(pe_units, U0["mix"] + m + 1)
                residual("mix", 0, m, None)
                finish("mix", 4, 0, m, lambda m: col("norm2", m))

            def ffn(i, j, ahead=True):
                if ahead:
                    split("ffn", i, j)
                t = 8 * i + (T0["ffn"] + j + 1)
                ve.wait_ge(pe_units, 8 * i + (U0["ffn"] + j + 1))
                ve.tensor_tensor(ab[:, j % 2, 0:SEQ], out_bank("ffn", j)[:, 0:SEQ], rstd[:, 0:SEQ], ALU.mult).then_inc(tile_read, 1)
                if j % 2 == 1:
                    m, b = 4 * i + j // 2, (j // 2) % 2
                    ve.wait_ge(tile_read, t)
                    ve.wait_ge(f_silu, m + 1)
                    ve.tensor_tensor(newt[:, b, :], ab[:, 1, 0:SEQ], sq[:, b, :], ALU.mult).then_inc(f_prod, 1)
                    ve.wait_ge(f_prod, m + 1)
                    ve.tensor_copy(chunk(f_hi, m), newt[:, b, :]).then_inc(f_hi_done, 1)
                    ve.wait_ge(f_hi_done, m + 1)
                    ve.tensor_tensor(chunk(f_lo, m), newt[:, b, :], chunk(f_hi, m).bitcast(F32), ALU.subtract).then_inc(f_lo_done, 1)

            split("ffn", 0, 0)
            norm(9, 8, rstd[:, 0:SEQ])
            for j in range(8):
                ffn(0, j, ahead=j > 0)
            with ve.Fori(1, 5) as i:
                for j in range(8):
                    ffn(i, j)
            for j in range(4):
                ffn(5, j)
            clear(5)
            for v in range(22):
                split("w2", v // 8, v % 8)
                if v in (11, 21):
                    ve.wait_ge(pe_units, U0["w2"] + v + (v == 21))
                    for m in range(4 * (v == 21), 4 * (v == 21) + 4):
                        residual("w2", 0, m, None)
                        finish("w2", 5, 0, m, None)
            norm(10, 9, rstd[:, 0:SEQ], banks[0])
            for m in range(DC):
                ve.scalar_tensor_tensor(yout[:, m, :], x[:, m, :], col("norm_f", m), rstd[:, 0:SEQ], ALU.mult, ALU.mult)\
                    .then_inc(yout_done, 1)


def bucket_table():
    t = np.zeros((33, 384), np.float32)
    for c in range(384):
        if c > 255:
            t[32, c] = 1.0
            continue
        dist = 255 - c
        if dist < 16:
            b = dist
        else:
            b = min(16 + int(np.float32(math.log(dist / 16)) / math.log(64) * 16 + 1e-6), 31)
        t[b, c] = 1.0
    return t


def columns(a, chunks=None):
    return np.ascontiguousarray(a.reshape(-1, P).T)


def tiles_of(w):
    k, m = w.shape
    return w.reshape(k // P, P, m // P, P).transpose(0, 2, 1, 3)


def stream(inputs):
    units = []

    def unit(tiles):
        block = np.zeros((P, UT, P), np.float32)
        for s, t in enumerate(tiles):
            block[:, s, :] = t
        units.append(block.reshape(P, UT * P))

    def by_output(w, order=None):
        t = tiles_of(w)
        for m in (range(t.shape[1]) if order is None else order):
            for k in range(0, t.shape[0], UT):
                unit([t[k + s, m] for s in range(UT)])

    def by_half(w):
        t = tiles_of(w)
        for h in range(2):
            for r in range(t.shape[0] // 2):
                unit([t[2 * r + s // 4, 4 * h + s % 4] for s in range(UT)])

    pool = [tiles_of(inputs["w_pool"][0, g]) for g in range(4)]
    for v in range(2):
        unit([pool[m // 2][kk, m % 2] for m in range(4 * v, 4 * v + 4) for kk in range(2)])
    by_output(inputs["w_up"][0])
    by_output(inputs["w_down"][0])
    by_output(inputs["w_qkv"][0], [8 * part + j for j in range(DC) for part in range(3)])
    by_output(inputs["w_o"][0])
    by_output(inputs["w_up"][1])
    by_output(inputs["w_down"][1])
    order = {"rx": range(16, 26), "glu": [x for m in range(8) for x in (m, 8 + m)], "rg": range(26, 36),
             "gb": range(44, 52), "ga": range(36, 44)}
    for name in ("rx", "glu", "rg"):
        by_output(inputs["w_in_2"][0], order[name])
    full = []
    for name in ("lru_wa_2", "lru_wx_2"):
        w = np.zeros((RC * P, RC * P), np.float32)
        for h in range(16):
            w[80 * h:80 * h + 80, 80 * h:80 * h + 80] = inputs[name][0, h]
        full.append(tiles_of(w))
    for v in range(GATE_UNITS):
        unit([full[g[1]][g[2], g[0]] for n, g in enumerate(GATES) if GATE_AT[n][0] == v])
    for name in ("gb", "ga"):
        by_output(inputs["w_in_2"][0], order[name])
    by_half(inputs["lru_w_out_2"][0])
    by_output(inputs["conv_w_out_2"][0])
    by_output(inputs["w_mix_out_2"][0])
    w1, w3 = tiles_of(inputs["ffn_w1_2"][0]), tiles_of(inputs["ffn_w3_2"][0])
    for m in range(F2C):
        unit([w1[k, m] for k in range(DC)])
        unit([w3[k, m] for k in range(DC)])
    by_half(inputs["ffn_w2_2"][0])
    assert len(units) == N_UNITS
    return np.stack(units).reshape(N_PAIRS, 2, P, UT * P).transpose(0, 2, 1, 3).reshape(N_PAIRS, P, PAIR)


def layouts(inputs):
    b_in = columns(inputs["b_in_2"][0])
    order = list(range(16, 26)) + [x for m in range(8) for x in (m, 8 + m)] + list(range(26, 52))
    mod = inputs["w_mod"].reshape(2, DC, P, 6, 4, 2 * P)[:, :, :, list(MOD_ORDER)]
    b_mod = inputs["b_mod"].reshape(2, 6, D)[:, list(MOD_ORDER)]
    parts = [("c", inputs["c"]), ("b_mod", b_mod), ("norm_mix", inputs["norm_mix"]), ("norm_mlp", inputs["norm_mlp"]),
             ("pool_scale", inputs["pool_scale"]), ("norm_final", inputs["norm_final"]), ("norm1", inputs["norm1_g_2"]),
             ("norm2", inputs["norm2_g_2"]), ("norm_f", inputs["norm_f_g_2"]), ("b_in", None),
             ("dw_w", inputs["conv_dw_w_2"]), ("dw_b", inputs["conv_dw_b_2"]), ("ln_g", inputs["conv_ln_g_2"]),
             ("ln_b", inputs["conv_ln_b_2"]), ("cb", inputs["conv_b_out_2"]), ("rw", inputs["lru_conv_w_2"]),
             ("rb", inputs["lru_conv_b_2"]), ("ba", inputs["lru_ba_2"]), ("bx", inputs["lru_bx_2"]),
             ("lam", inputs["lru_lambda_2"])]
    assert [p[0] for p in parts] == list(VEC)
    vectors = np.concatenate([b_in[:, order] if a is None else columns(np.asarray(a)) for _, a in parts], axis=1)
    assert vectors.shape == (P, NVEC)
    return {
        "weights": stream(inputs),
        "w_mod": np.ascontiguousarray(mod.transpose(0, 3, 4, 2, 1, 5).reshape(MODS, P, DC * SEQ)),
        "x_in": np.ascontiguousarray(inputs["x"][0].T.reshape(DC, P, SEQ).transpose(1, 0, 2)),
        "vectors": np.ascontiguousarray(vectors),
        "rel_bias": np.ascontiguousarray(inputs["rel_bias"]),
        "buckets": bucket_table(),
        "inv_count": (1.0 / np.minimum(np.arange(1, SEQ + 1)[None, :], np.array(WINDOWS)[:, None])).astype(np.float32),
        "identity": np.eye(P, dtype=np.float32),
    }


def kernel(**inputs):
    import concourse.bacc as bacc
    from concourse.bass_utils import run_bass_kernel_spmd

    inputs = {k: np.asarray(v) for k, v in inputs.items()}
    arrays = layouts(inputs)
    nc = bacc.Bacc("TRN2", target_bir_lowering=False, num_devices=1)
    args = [nc.dram_tensor(k, a.shape, mybir.dt.from_np(a.dtype), kind="ExternalInput").ap() for k, a in arrays.items()]
    out = nc.dram_tensor("y_out", (D, SEQ), F32, kind="ExternalOutput").ap()
    build(nc, *args, out)
    got = run_bass_kernel_spmd(nc, [arrays], core_ids=[0]).results[0]["y_out"]
    return np.ascontiguousarray(np.asarray(got).T)[None]
```

```python
from contextlib import ExitStack, contextmanager
import math

import numpy as np

import concourse.bass as bass
from concourse import mybir

ALU = mybir.AluOpType
ACT = mybir.ActivationFunctionType
AX = mybir.AxisListType
F32 = mybir.dt.float32
F32R = mybir.dt.float32r

P = 128
SEQ = 256
D = 1024
DC = D // P
FFC = 4 * D // P
RC = 1280 // P
F2C = 2816 // P
HEADS, HD = 16, 64
EPS = 1e-6
WINDOWS = (2, 4, 8, 16)
TAPS, RTAPS = 31, 4
UT = 8
PAIR = 2 * UT * P
RAW = 4
HL = 4
HI_LEAD = 4
LO_LEAD = 3

PHASES = [("pool", 2, 8), ("up0", 32, 32), ("down0", 32, 8), ("qkv", 24, 24), ("o", 8, 8),
          ("up1", 32, 32), ("down1", 32, 8), ("glu", 16, 16), ("rx", 10, 10), ("rg", 10, 10),
          ("gates", 8, 20), ("gb", 8, 8), ("ga", 8, 8), ("lru", 10, 8), ("conv", 8, 8),
          ("mix", 8, 8), ("ffn", 44, 44), ("w2", 22, 8)]
GLU_SPLIT = 8
WHOLE = ("rg", "gb", "ga", "lru")
ACT_READS = ("rg", "gates", "gb", "ga")

U0, B0, T0, A0, NATIVE = {}, {}, {}, {}, set()


def _phases():
    units = tiles = by_vector = by_scalar = 0
    for name, u, t in PHASES:
        U0[name], B0[name], T0[name], A0[name] = units, tiles, by_vector, by_scalar
        if name == "glu":
            NATIVE.update(range(units + GLU_SPLIT, units + u))
        if name in WHOLE:
            NATIVE.update(range(units, units + u))
        units, tiles = units + u, tiles + t
        if name in ACT_READS:
            by_scalar += t
        else:
            by_vector += GLU_SPLIT if name == "glu" else t
    return units


N_UNITS = _phases()
N_PAIRS = N_UNITS // 2


def splits(u):
    return u + 1 - sum(n <= u for n in NATIVE)


def count_of(name, i, j):
    if isinstance(i, int):
        return splits(U0[name] + 8 * i + j)
    return 8 * i + splits(U0[name] + j)


SC1, SH1, G1, SC2, SH2, G2 = range(6)
MOD_ORDER = (1, 0, 2, 4, 3, 5)
MODS = 48
MOD_FIRST = 20
MOD_POOL = 16



def second_half(chunks):
    return [(m, k) for m in range(4, 8) for k in range(chunks)]


LRU_TILES, LAST_TILES = second_half(RC), second_half(F2C)
LRU_UNIT, LAST_UNIT = ({m: len(t) // UT + max(n for n, mk in enumerate(t) if mk[0] == m) // UT for m in range(4, 8)}
                       for t in (LRU_TILES, LAST_TILES))
W2_DONE = {11: (0, 1), 12: (2, 3)}
W2_DONE.update({min(LAST_UNIT[m] + 1, 21): (m,) for m in range(4, 8)})

VEC = {}


def _columns():
    at = 0
    for name, k in (("c", DC), ("b_mod", 96), ("norm_mix", 16), ("norm_mlp", 16), ("pool_scale", 8),
                    ("norm_final", 8), ("norm1", 8), ("norm2", 8), ("norm_f", 8), ("b_in", 52),
                    ("dw_w", TAPS * DC), ("dw_b", DC), ("ln_g", DC), ("ln_b", DC), ("cb", DC),
                    ("rw", RTAPS * RC), ("rb", RC), ("ba", RC), ("bx", RC), ("lam", RC)):
        VEC[name] = at
        at += k
    return at


NVEC = _columns()


def gate_tiles():
    return [sorted({r // P for h in range(m * P // 80, (m * P + P - 1) // 80 + 1)
                    for r in range(80 * h, 80 * h + 80)}) for m in range(RC)]


def gate_stream():
    out = []
    for m, ks in enumerate(gate_tiles()):
        for which in range(2):
            out += [(m, which, k, k == ks[0], k == ks[-1]) for k in ks]
    return out


GATES = gate_stream()
GATE_UNITS = 8
LAST_TAPS = (TAPS - 1) * DC
REC_AT = (1, 3, 5, 7, 9, 10, 11, 12, 13, 14)
MULT_AT = 3
HB_AT = (6, 7, 8, 9, 10, 11, 12, 13, 14, 15)
TAPS_AT = {"glu": [0, 0, 0, 0, 1, 1, 1, 1] + 5 * [7] + 3 * [4],
           "rx": 5 * [3, 0] + 5 * [4] + 2 * [8] + 3 * [5],
           "gates": 5 * [3] + 3 * [5],
           "gb": [1, 9, 9, 1, 9, 1, 7, 7] + 8 * [6]}
TAPS_AT["gb"][-1] = LAST_TAPS
GATE_AT = [(n * GATE_UNITS // len(GATES),
            n - sum(t * GATE_UNITS // len(GATES) < n * GATE_UNITS // len(GATES) for t in range(len(GATES))))
           for n in range(len(GATES))]
GATE_DONE = [GATE_AT[n][0] for n, g in enumerate(GATES) if g[4]]


def mod_slot(q):
    return q % 4 if q < MOD_FIRST else q % 2


def mod_landed(q):
    return 16 * sum(mod_slot(r) == mod_slot(q) for r in range(q + 1))


def build(nc, weights, w_mod, x_in, vectors, rel_bias, buckets, inv_count, identity, out):
    scratch = nc.dram_tensor("bias_by_distance", [HEADS, 384], F32, kind="Internal").ap()
    with ExitStack() as ctx:
        def sb(name, shape, dt=F32, where=ctx):
            return where.enter_context(nc.sbuf_tensor(name, shape, dt))

        def sem(name):
            return ctx.enter_context(nc.semaphore(name))

        raw = sb("raw", [P, RAW, PAIR])
        w_hi = sb("w_hi", [P, HL, UT * P], F32R)
        w_lo = sb("w_lo", [P, HL, UT * P], F32R)
        x = sb("x", [P, DC, SEQ])
        with ExitStack() as part:
            xg_hi = sb("xg_hi", [P, DC, SEQ + 2], F32R, part)
        h32b = sb("h32b", [P, DC, SEQ + 2])
        xg_lo = sb("xg_lo", [P, DC, SEQ + 2], F32R)
        vec = sb("vec", [P, NVEC])
        modv = sb("modv", [P, 96])
        gain = sb("gain", [P, 4, DC])
        gate0 = sb("gate0", [P, DC])
        gain1 = sb("gain1", [P, DC])
        ones = sb("ones", [P, P])
        ident = sb("ident", [P, P])
        rstd = sb("rstd", [P, SEQ + 2])
        rstd1 = sb("rstd1", [P, SEQ])
        var = sb("var", [P, SEQ])
        newt = sb("newt", [P, 2, SEQ])
        acc = sb("acc", [P, SEQ])
        acc2 = sb("acc2", [P, SEQ])
        sq = sb("sq", [P, 2, SEQ])
        ab = sb("ab", [P, 2, SEQ + 2])
        sp = sb("sp", [P, 8, RC])

        first = ExitStack()
        cz = sb("cz", [P, DC, 32], F32, first)
        mod_raw = sb("mod_raw", [P, 4, DC * SEQ], F32, first)
        mod_row = sb("mod_row", [P, 2, SEQ], F32, first)
        ub = sb("ub", [P, 2, SEQ], F32, first)
        sb2 = sb("sb2", [P, 2, SEQ], F32, first)
        with ExitStack() as part:
            PADW = SEQ + 16
            h_pad = sb("h_pad", [P, DC, PADW], F32, part)
            s2 = sb("s2", [P, DC, PADW], F32, part)
            s4 = sb("s4", [P, 6, PADW], F32, part)
            s8 = sb("s8", [P, 4, PADW], F32, part)
            s16 = sb("s16", [P, 2, PADW], F32, part)
            invc = sb("invc", [P, 4, SEQ], F32, part)
            rbx = sb("rbx", [33, HEADS], F32, part)
            bkt = sb("bkt", [33, 384], F32, part)
            bydist = sb("bydist", [HEADS, 384], F32, part)
            pool_hi = sb("pool_hi", [P, DC, SEQ], F32R, part)
            pool_lo = sb("pool_lo", [P, DC, SEQ], F32R, part)
        with ExitStack() as part:
            hid_hi = sb("hid_hi", [P, FFC, SEQ], F32R, part)
            hid_lo = sb("hid_lo", [P, FFC, SEQ], F32R, part)
        with ExitStack() as part:
            qT = sb("qT", [P, 2, SEQ], F32, part)
            kT = sb("kT", [P, 2, SEQ], F32, part)
            vT = sb("vT", [P, 2, SEQ], F32, part)
            vtok = sb("vtok", [P, 2, SEQ], F32, part)
            toep = sb("toep", [P, 2, 2, 384], F32, part)
            logit = sb("logit", [P, 2, 384], F32, part)
            prob = sb("prob", [P, 2, 384], F32, part)
            probn = sb("probn", [P, 2, 384], F32, part)
            pT = sb("pT", [P, 2, 384], F32, part)
            smx = sb("smx", [P, 2, 8], F32, part)
            o_hi = sb("o_hi", [P, DC, SEQ], F32R, part)
            o_lo = sb("o_lo", [P, DC, SEQ], F32R, part)
        first.close()
        with ExitStack() as part:
            RXW = SEQ + RTAPS - 1
            UW = SEQ + TAPS - 1
            rx = sb("rx", [P, RC, RXW], F32, part)
            with ExitStack() as inner:
                act_hi = sb("act_hi", [P, RC, SEQ], F32R, inner)
                act_lo = sb("act_lo", [P, RC, SEQ], F32R, inner)
            a2 = sb("a2", [P, RC, SEQ], F32, part)
            sb("behind_a2", [P, RC, SEQ], F32, part)
            u = sb("u", [P, DC, UW], F32, part)
            y = sb("y", [P, DC, SEQ], F32, part)
            grg = sb("grg", [P, RC, SEQ], F32, part)
            rt = sb("rt", [P, RC, SEQ], F32, part)
            ig = sb("ig", [P, RC, SEQ], F32, part)
            av = sb("av", [P, RC, SEQ], F32, part)
            sga = sb("sga", [P, DC, SEQ], F32, part)
            h32 = sga
            sgb = sb("sgb", [P, DC, SEQ], F32, part)
        with ExitStack() as part:
            f_hi = sb("f_hi", [P, F2C, SEQ], F32R, part)
            f_lo = sb("f_lo", [P, F2C, SEQ], F32R, part)
            yout = sb("yout", [P, DC, SEQ], F32, part)

        banks = [ctx.enter_context(nc.psum_tensor(f"bank{b}", [P, 512], F32)) for b in range(8)]
        row_banks, col_banks, stat_bank = (banks[4], banks[6]), (banks[5], banks[7]), banks[6]
        s_bank, t_bank, o_bank = banks[6], banks[7], banks[3]

        landed = [sem(f"landed{k}") for k in range(RAW)]
        hi_done = sem("hi_done")
        lo_done = sem("lo_done")
        pe_units = sem("pe_units")
        tile_read = sem("tile_read")
        mod_in = [sem(f"mod_in{k}") for k in range(4)]
        mod_rows = sem("mod_rows")
        mod_copied = sem("mod_copied")
        mod_cols = sem("mod_cols")
        mod_read = sem("mod_read")
        x_in_s, vec_in, small_in, inv_in = sem("x_in_s"), sem("vec_in"), sem("small_in"), sem("inv_in")
        consts = sem("consts")
        pads = sem("pads")
        c_act = sem("c_act")
        x_sq = sem("x_sq")
        dve = sem("dve_chain")
        stat_in = sem("stat_in")
        stat_mm = sem("stat_mm")
        var_done = sem("var_done")
        root_done = sem("root_done")
        gain_done = sem("gain_done")
        xr_done = sem("xr_done")
        h_done = sem("h_done")
        pool_in = sem("pool_in")
        shift_done = sem("shift_done")
        sq_done = sem("sq_done")
        acc_done = sem("acc_done")
        acc2_done = sem("acc2_done")
        xg_hi_done = sem("xg_hi_done")
        xg_lo_done = sem("xg_lo_done")
        relu_done = sem("relu_done")
        sq2_done = sem("sq2_done")
        hid_hi_done = sem("hid_hi_done")
        hid_lo_done = sem("hid_lo_done")
        bias_mm, bias_cp, bias_out = sem("bias_mm"), sem("bias_cp"), sem("bias_out")
        toep_in = [sem("toep_in0"), sem("toep_in1")]
        qkv_done = sem("qkv_done")
        score_done = sem("score_done")
        logit_done = sem("logit_done")
        max_done = sem("max_done")
        neg_done = sem("neg_done")
        exp_done = sem("exp_done")
        prob_done = sem("prob_done")
        pt_done = sem("pt_done")
        pt_copied = sem("pt_copied")
        vt_done = sem("vt_done")
        vt_copied = sem("vt_copied")
        pv_done = sem("pv_done")
        o_hi_done = sem("o_hi_done")
        o_lo_done = sem("o_lo_done")
        z_done = sem("z_done")
        xb_done = sem("xb_done")
        act_hi_done = sem("act_hi_done")
        act_lo_done = sem("act_lo_done")
        h32_done = sem("h32_done")
        h32_moved = sem("h32_moved")
        rtap_done = sem("rtap_done")
        ytap_done = sem("ytap_done")
        u_done = sem("u_done")
        tap_done = sem("tap_done")
        act_read = sem("act_read")
        decay_done = sem("decay_done")
        mult2_done = sem("mult2_done")
        mult_done = sem("mult_done")
        hb_done = sem("hb_done")
        ln_sq, ln_silu, ln_hi, ln_lo = sem("ln_sq"), sem("ln_silu"), sem("ln_hi"), sem("ln_lo")
        ln_c, ln_n = sem("ln_c"), sem("ln_n")
        m_done = sem("m_done")
        f_silu, f_prod, f_hi_done, f_lo_done = sem("f_silu"), sem("f_prod"), sem("f_hi_done"), sem("f_lo_done")
        yout_done, stored = sem("yout_done"), sem("stored")

        def col(name, k, n=1):
            return vec[:, VEC[name] + k:VEC[name] + k + n]

        def loop_units(eng, name, step, end=None):
            n = PHASES[[p[0] for p in PHASES].index(name)][1] if end is None else end
            full = n // 8
            if full > 1:
                with eng.Fori(0, full) as i:
                    for j in range(8):
                        step(i, j)
                tail = range(8 * full, n)
            else:
                tail = range(n)
            for v in tail:
                step(v // 8, v % 8)

        def out_bank(name, v):
            if name in ("down0", "down1"):
                return banks[v % 2]
            if name == "qkv":
                return banks[v % 3]
            if name == "w2":
                return banks[v]
            if name == "lru" and 4 <= v < 7:
                return (banks[4], banks[5], banks[7])[v - 4]
            return banks[(B0[name] + v) % 4]

        def freed(name, v):
            v -= 4
            if v < 0:
                at = [p[0] for p in PHASES].index(name) - 1
                name = PHASES[at][0]
                v += PHASES[at][2]
            if name == "glu" and v >= GLU_SPLIT:
                return u_done, v // 2 + 1
            if name in ACT_READS:
                return act_read, A0[name] + v + 1
            return tile_read, T0[name] + v + 1

        def one(i, k=1):
            return bass.ds(i, k) if not isinstance(i, int) else slice(i, i + k)

        def chunk(t, i, w=SEQ):
            return t[:, one(i), 0:w].rearrange("p a n -> p (a n)")

        def reverse(t):
            step, count = t.ap[0]
            return bass.AP(t.tensor, t.offset + P - 1, [[step, count], [P, 2], [-1, P]])

        block = ctx.enter_context(nc.Block())

        @block.sync
        def _(sp):
            sp.dma_start(x[:], x_in).then_inc(x_in_s, 16)
            sp.dma_start(vec[:], vectors).then_inc(vec_in, 16)

            def piece(q, s):
                if not isinstance(q, int) or q >= 4:
                    sp.wait_ge(mod_rows, q - (3 if isinstance(q, int) and q < MOD_FIRST else 1))
                sp.dma_start(mod_raw[:, s, :], w_mod[one(q)].rearrange("a p n -> p (a n)")).then_inc(mod_in[s], 16)

            def pair(p, s, base=0):
                if not isinstance(p, int):
                    sp.wait_ge(lo_done, 2 * (p - RAW) + 2 - base)
                elif p >= RAW and 2 * (p - RAW) in NATIVE:
                    sp.wait_ge(pe_units, 2 * (p - RAW) + 2)
                elif p >= RAW:
                    sp.wait_ge(lo_done, splits(2 * (p - RAW) + 1))
                sp.dma_start(raw[:, s, :], weights[one(p)].rearrange("a p n -> p (a n)")).then_inc(landed[s], 16)

            for q in range(4):
                piece(q, q)
            sp.dma_start(rbx[0:32, :], rel_bias).then_inc(small_in, 16)
            sp.dma_start(bkt[:], buckets).then_inc(small_in, 16)
            sp.dma_start(ident[:], identity).then_inc(small_in, 16)
            sp.dma_start(invc[:], bass.AP(inv_count.tensor, 0, [[0, P], [SEQ, 4], [1, SEQ]])).then_inc(inv_in, 16)
            for q in range(4, 12):
                piece(q, mod_slot(q))
                if q == 7:
                    pair(0, 0)
            sp.wait_ge(bias_cp, 1)
            sp.dma_start(scratch, bydist[:]).then_inc(bias_out, 16)
            for q in range(12, MOD_FIRST):
                piece(q, mod_slot(q))
            def mlp_loads(i):
                for s in range(4):
                    pair(4 * i + 1 + s, (1 + s) % RAW)
                    if s >= 2:
                        piece(2 * i + MOD_FIRST + s - 2, s - 2)

            mlp_loads(0)
            with sp.Fori(1, 8) as i:
                mlp_loads(i)

            def toeplitz(a):
                if a >= 2:
                    sp.wait_ge(logit_done, 2 * (a - 2) + 2)
                for seg, base in ((slice(0, 128), 128), (slice(128, 384), 0)):
                    src = bass.AP(scratch.tensor, base + 2 * 384 * a,
                                  [[1, P], [384, 2], [1, seg.stop - seg.start]])
                    sp.dma_start(toep[:, a % 2, :, seg], src).then_inc(toep_in[a % 2], 16)

            sp.wait_ge(bias_out, 16)
            p0 = U0["qkv"] // 2
            for n in range(12):
                pair(p0 + n, (p0 + n) % RAW)
                if n == 3:
                    sp.wait_ge(pe_units, U0["qkv"])
                for a in range(DC):
                    if n == max(3, min(11, (3 * a + 1) // 2 + 1)):
                        toeplitz(a)
                for q in range(DC):
                    if n == max(1, (3 * q - 2) // 2 + 1):
                        piece(36 + q, q % 2)
            for a in range(4):
                pair(p0 + 12 + a, (p0 + 12 + a) % RAW)
                piece(44 + a, a % 2)
            p0 += 16
            loops = (U0["glu"] // 2 - p0) // RAW
            with sp.Fori(0, loops) as i:
                for s in range(RAW):
                    pair(4 * i + p0 + s, (p0 + s) % RAW)
            p1 = p0 + RAW * loops
            p0 = N_PAIRS - (N_PAIRS - (max(NATIVE) + 1) // 2 - RAW) // RAW * RAW
            for p in range(p1, p0):
                pair(p, p % RAW)
            with sp.Fori(0, (N_PAIRS - p0) // RAW) as i:
                for s in range(RAW):
                    pair(4 * i + p0 + s, (p0 + s) % RAW, len(NATIVE))
            for m in range(DC):
                sp.wait_ge(yout_done, m + 1)
                sp.dma_start(out[m * P:(m + 1) * P, :], yout[:, m, :]).then_inc(stored, 16)
            sp.wait_ge(stored, 16 * DC)

        @block.gpsimd
        def _(pool):
            nc.gpsimd.memset(cz[:], 0.0).then_inc(consts, 1)
            nc.gpsimd.memset(ones[:], 1.0).then_inc(consts, 1)
            nc.gpsimd.memset(rstd[:, SEQ:SEQ + 2], 1.0).then_inc(consts, 1)
            pool.wait_ge(consts, 3)
            nc.gpsimd.memset(rbx[32:33, :], -1e30).then_inc(consts, 1)
            pool.wait_ge(consts, 4)
            for t in (h_pad, s2, s4, s8):
                nc.gpsimd.memset(t[:, :, 0:16], 0.0).then_inc(consts, 1)
            pool.wait_ge(pe_units, U0["glu"])
            nc.gpsimd.memset(rx[:, :, 0:RTAPS - 1], 0.0).then_inc(pads, 1)
            nc.gpsimd.memset(u[:, :, 0:TAPS - 1], 0.0).then_inc(pads, 1)

        @block.tensor
        def _(pe):
            def product(dst, slot, s, r_hi, r_lo, start, stop):
                hi = w_hi[:, slot, s * P:(s + 1) * P]
                lo = w_lo[:, slot, s * P:(s + 1) * P]
                pe.matmul(dst, hi, r_hi, start=start, stop=False, skip_group_check=True)
                pe.matmul(dst, hi, r_lo, start=False, stop=False, skip_group_check=True)
                return pe.matmul(dst, lo, r_hi, start=False, stop=stop, skip_group_check=True)

            def unit_ready(name, i, j):
                pe.wait_ge(hi_done, count_of(name, i, j))
                pe.wait_ge(lo_done, count_of(name, i, j))

            def rows(q, s, ready):
                pe.wait_ge(mod_in[s], ready)
                if isinstance(q, int) and q < MOD_FIRST:
                    if q == 1:
                        pe.wait_ge(var_done, 1)
                    if q >= 2:
                        pe.wait_ge(mod_copied, q - 1)
                else:
                    pe.wait_ge(mod_copied, q)
                row_bank = row_banks[q % 2 if isinstance(q, int) and q < MOD_FIRST else 0]
                for k in range(DC):
                    g = k % 4
                    mm = pe.matmul(row_bank[32 * g:32 * g + 32, 0:SEQ], cz[:, k, :], mod_raw[:, s, SEQ * k:SEQ * (k + 1)],
                                   start=k < 4, stop=k >= 4, tile_position=(0, 32 * g))
                mm.then_inc(mod_rows, 1)

            def cols(q, s):
                pe.wait_ge(mod_copied, q + 1)
                if isinstance(q, int) and q < MOD_FIRST:
                    g = q // 4
                    dst, at = col_banks[g % 2], 2 * (q % 4)
                    if g >= 2:
                        pe.wait_ge(mod_read, g - 1)
                else:
                    dst, at = col_banks[0], 0
                    pe.wait_ge(mod_read, q - (MOD_FIRST - 5))
                for half in range(2):
                    mm = pe.matmul(dst[:, at + half:at + half + 1], mod_row[:, s, half * P:(half + 1) * P],
                                   ones[:, 0:1], start=True, stop=True)
                mm.then_inc(mod_cols, 1)

            def stats(ready, src, at=0, dst=stat_bank):
                pe.wait_ge(*ready)
                pe.matmul(dst[:, at:at + SEQ], ones[:], src[:], start=True, stop=True).then_inc(stat_mm, 1)

            pe.wait_ge(consts, 8)
            pe.wait_ge(c_act, 1)
            stats((stat_in, 1), acc)
            for q in range(MOD_POOL):
                rows(q, q % 4, mod_landed(q))
                if q == 3:
                    pe.wait_ge(small_in, 48)
                    pe.matmul(banks[0][0:HEADS, 0:384], rbx[:], bkt[:], start=True, stop=True).then_inc(bias_mm, 1)
                if q:
                    cols(q - 1, (q - 1) % 2)
            cols(MOD_POOL - 1, (MOD_POOL - 1) % 2)
            pe.wait_ge(bias_cp, 1)
            for v in range(2):
                unit_ready("pool", 0, v)
                for mi in range(4):
                    m = 4 * v + mi
                    pe.wait_ge(pool_in, m // 2 + 1)
                    if m >= 4:
                        pe.wait_ge(tile_read, m - 3)
                    for kk in range(2):
                        k = 2 * (m // 2) + kk
                        mm = product(out_bank("pool", m)[:, 0:SEQ], v % HL, 2 * mi + kk, pool_hi[:, k, :], pool_lo[:, k, :],
                                     kk == 0, kk == 1)
                mm.then_inc(pe_units, 1)
            for q in range(MOD_POOL, MOD_FIRST):
                rows(q, q % 4, mod_landed(q))
                if q > MOD_POOL:
                    cols(q - 1, (q - 1) % 2)
            cols(MOD_FIRST - 1, (MOD_FIRST - 1) % 2)

            def whole(name, i, j, r_hi, r_lo, n, ready=None):
                unit_ready(name, i, j)
                if name == "qkv":
                    pe.wait_ge(tile_read, T0[name] + 8 * i + j - 2)
                elif name in ("rx", "conv", "mix") or name == "glu" and 8 * i + j >= 4:
                    pe.wait_ge(*freed(name, 8 * i + j))
                else:
                    pe.wait_ge(tile_read, 8 * i + (T0[name] + j - 3))
                dst = out_bank(name, 8 * i + j if name == "qkv" else j)
                for k in range(DC):
                    if j == 0 and ready is not None:
                        pe.wait_ge(ready[0], ready[1] + k + 1)
                    mm = product(dst[:, 0:n], (U0[name] + j) % HL, k, r_hi[:, k, 0:n], r_lo[:, k, 0:n], k == 0, k == DC - 1)
                mm.then_inc(pe_units, 1)

            def with_piece(i, j, base):
                if j % 4 == 2:
                    rows(2 * i + (MOD_FIRST + base + j // 4), j // 4, 16 * i + (landed_base(j // 4) + 16 + 16 * (base // 2)))
                if j % 4 == 3:
                    cols(2 * i + (MOD_FIRST + base + j // 4), j // 4)

            def landed_base(s):
                return 16 * sum(mod_slot(q) == s for q in range(MOD_FIRST))

            def down(name, i, j):
                unit_ready(name, i, j)
                base = 0 if name == "down0" else 32
                dst = out_bank(name, j // 4)
                if j % 4 == 0:
                    pe.wait_ge(tile_read, 2 * i + (T0[name] + j // 4 - 1))
                for s in range(UT):
                    k = 8 * (j % 4) + s
                    if j < 4:
                        pe.wait_ge(hid_lo_done, base + k + 1)
                    mm = product(dst[:, 0:SEQ], (U0[name] + j) % HL, s, hid_hi[:, k, :], hid_lo[:, k, :], k == 0, k == FFC - 1)
                mm.then_inc(pe_units, 1)
                if name == "down0":
                    with_piece(i, j, 8)

            def first_down(name):
                pe.wait_ge(tile_read, T0[name])
                loop_units(pe, name, lambda i, j: down(name, i, j))

            def up_phase(name):
                pe.wait_ge(tile_read, T0[name])
                sums = (acc_done, 8 if name == "up0" else 26)
                pe.wait_ge(shift_done, 1 if name == "up0" else 3)

                def step(i, j):
                    whole(name, i, j, xg_hi, xg_lo, SEQ + 2, (xg_lo_done, 0 if name == "up0" else 16))
                    if name == "up0":
                        with_piece(i, j, 0)
                for j in range(8):
                    step(0, j)
                    if j == 0:
                        stats(sums, acc)
                with pe.Fori(1, 4) as i:
                    for j in range(8):
                        step(i, j)

            up_phase("up0")
            first_down("down0")

            def scores(a, e):
                pe.wait_ge(qkv_done, 3 * a + 2)
                if 2 * a + e:
                    pe.wait_ge(logit_done, 2 * a + e)
                else:
                    pe.wait_ge(var_done, 3)
                r = slice(64 * e, 64 * e + 64)
                pe.matmul(s_bank[:, 0:128], qT[r, a % 2, 0:128], kT[r, a % 2, 0:128], start=True, stop=True)
                pe.matmul(s_bank[:, 128:384], qT[r, a % 2, 128:256], kT[r, a % 2, :], start=True, stop=True)\
                    .then_inc(score_done, 1)

            def values(a):
                pe.wait_ge(qkv_done, 3 * a + 3)
                if a:
                    pe.wait_ge(pt_copied, 2 * a)
                pe.transpose(t_bank[:, 0:128], vT[:, a % 2, 0:128], ident[:])
                pe.transpose(t_bank[:, 128:256], vT[:, a % 2, 128:256], ident[:]).then_inc(vt_done, 1)

            def turn(a, e):
                pe.wait_ge(prob_done, 2 * a + e + 1)
                if e == 0:
                    pe.wait_ge(vt_copied, a + 1)
                else:
                    pe.wait_ge(pt_copied, 2 * a + 1)
                for b in range(3):
                    mm = pe.transpose(t_bank[:, b * P:(b + 1) * P], probn[:, e, b * P:(b + 1) * P], ident[:])
                mm.then_inc(pt_done, 1)

            def weigh(a):
                pe.wait_ge(pt_copied, 2 * a + 2)
                if a:
                    pe.wait_ge(o_lo_done, a)
                for e in range(2):
                    dst = o_bank[64 * e:64 * e + 64, :]
                    pe.matmul(dst[:, 0:256], vtok[:, a % 2, 64 * e:64 * e + 64], pT[:, e, 0:256], start=True, stop=False,
                              skip_group_check=True)
                    mm = pe.matmul(dst[:, 128:256], vtok[:, a % 2, 128 + 64 * e:192 + 64 * e], pT[:, e, 256:384],
                                   start=False, stop=True, skip_group_check=True)
                mm.then_inc(pv_done, 1)

            def o_part(j, chunks):
                unit_ready("o", 0, j)
                pe.wait_ge(tile_read, T0["o"] + max(0, j - 3))
                for k in chunks:
                    pe.wait_ge(o_lo_done, k + 1)
                    mm = product(out_bank("o", j)[:, 0:SEQ], (U0["o"] + j) % HL, k, o_hi[:, k, :], o_lo[:, k, :], k == 0, k == DC - 1)
                    if k == DC - 1:
                        mm.then_inc(pe_units, 1)

            pe.wait_ge(tile_read, T0["qkv"])
            pe.wait_ge(shift_done, 2)
            for j in range(DC + 2):
                a = j - 1
                for part in range(3):
                    v = 3 * j + part
                    if j < DC:
                        whole("qkv", v // 8, v % 8, xg_hi, xg_lo, SEQ + 2, (xg_lo_done, 8))
                    if v == 0:
                        stats((acc_done, 17), acc)
                    if part == 0:
                        if 0 <= a < DC:
                            scores(a, 0)
                        if 1 <= a <= DC:
                            turn(a - 1, 1)
                        if j <= DC:
                            rows(36 + j, j % 2, mod_landed(36 + j))
                        if j == DC:
                            o_part(0, range(0, 6))
                        if j == DC + 1:
                            o_part(0, (6,))
                            o_part(1, (6,))
                            o_part(2, range(0, 7))
                    if part == 1:
                        if 0 <= a < DC:
                            scores(a, 1)
                        if 1 <= a <= DC:
                            weigh(a - 1)
                        if 0 <= a < DC:
                            values(a)
                        if j <= DC:
                            cols(36 + j, j % 2)
                        if j == DC:
                            o_part(1, range(0, 6))
                    if part == 2 and 0 <= a < DC:
                        turn(a, 0)

            for j in range(8):
                o_part(j, (7,) if j < 3 else range(DC))
                if j % 2 == 0 and j < 6:
                    rows(45 + j // 2, (j // 2 + 1) % 2, mod_landed(45 + j // 2))
                if j % 2 == 1 and j < 6:
                    cols(45 + j // 2, (j // 2 + 1) % 2)
            up_phase("up1")
            first_down("down1")

            def native(name, v, src):
                at = U0[name] + v
                slot = (at // 2) % RAW
                pe.wait_ge(landed[slot], 16 * (at // 8 + 1))
                pe.wait_ge(*freed(name, v))
                for k in range(DC):
                    mm = pe.matmul(out_bank(name, v)[:, 0:SEQ], raw[:, slot, ((at % 2) * UT + k) * P:((at % 2) * UT + k + 1) * P],
                                   src[:, k, 0:SEQ], start=k == 0, stop=k == DC - 1)
                mm.then_inc(pe_units, 1)

            pe.wait_ge(tile_read, T0["glu"])
            for v in range(16):
                if v < GLU_SPLIT:
                    whole("glu", v // 8, v % 8, xg_hi, xg_lo, SEQ, (xg_lo_done, 24) if v == 0 else None)
                else:
                    if v == GLU_SPLIT:
                        pe.wait_ge(h32_done, DC)
                    native("glu", v, h32)
                if v == 0:
                    stats((acc_done, 35), acc)
                    stats((acc2_done, 9), acc2, SEQ)
            for v in range(10):
                whole("rx", v // 8, v % 8, xg_hi, xg_lo, SEQ)
            for v in range(10):
                native("rg", v, h32)
            g = 0
            for n, (m, which, k, start, stop) in enumerate(GATES):
                w, s = GATE_AT[n]
                if s == 0:
                    unit_ready("gates", 0, w)
                if start:
                    pe.wait_ge(act_lo_done, max(gate_tiles()[m]) + 1)
                    pe.wait_ge(*freed("gates", g))
                mm = product(out_bank("gates", g)[:, 0:SEQ], (U0["gates"] + w) % HL, s, act_hi[:, k, :], act_lo[:, k, :],
                             start, stop)
                g += stop
                if n == len(GATES) - 1 or GATE_AT[n + 1][1] == 0:
                    mm.then_inc(pe_units, 1)
            pe.wait_ge(h32_moved, 1)
            for name in ("gb", "ga"):
                for v in range(8):
                    native(name, v, h32b)

            def lru(v):
                at, q = U0["lru"] + v, v % 5
                slot = (at // 2) % RAW
                pe.wait_ge(landed[slot], 16 * (at // 8 + 1))
                if v < 5:
                    pe.wait_ge(hb_done, q + 1)
                for s in range(UT):
                    m, k = (s % 4, 2 * q + s // 4) if v < 5 else LRU_TILES[UT * q + s]
                    if k == 0 and (m < 4 or m == 7):
                        pe.wait_ge(*freed("lru", m))
                    mm = pe.matmul(out_bank("lru", m)[:, 0:SEQ], raw[:, slot, ((at % 2) * UT + s) * P:((at % 2) * UT + s + 1) * P],
                                   rt[:, k, :], start=k == 0, stop=k == RC - 1, skip_group_check=True)
                mm.then_inc(pe_units, 1)

            for v in range(10):
                lru(v)
                if v == 0:
                    stats((stat_in, 2), acc2)
                if v == 3:
                    stats((stat_in, 3), acc2)
            for j in range(8):
                whole("conv", 0, j, xg_hi, xg_lo, SEQ, (ln_lo, 0))
            for j in range(8):
                whole("mix", 0, j, act_hi, act_lo, SEQ, (act_lo_done, RC))
            for j in range(8):
                whole("ffn", 0, j, xg_hi, xg_lo, SEQ, (xg_lo_done, 32))
                if j == 0:
                    stats((acc_done, 44), acc)
            with pe.Fori(1, 5) as i:
                for j in range(8):
                    whole("ffn", i, j, xg_hi, xg_lo, SEQ)
            for j in range(4):
                whole("ffn", 5, j, xg_hi, xg_lo, SEQ)
            for v in range(11):
                unit_ready("w2", 0, v)
                for s in range(UT):
                    k, m = 2 * v + s // 4, s % 4
                    if m == 0:
                        pe.wait_ge(f_lo_done, k + 1)
                    if k == 0:
                        pe.wait_ge(tile_read, T0["w2"])
                    mm = product(banks[m][:, 0:SEQ], (U0["w2"] + v) % HL, s, f_hi[:, k, :], f_lo[:, k, :], k == 0, k == F2C - 1)
                mm.then_inc(pe_units, 1)
            for v in range(11, 22):
                unit_ready("w2", 0, v)
                for s in range(UT):
                    m, k = LAST_TILES[UT * (v - 11) + s]
                    mm = product(banks[m][:, 0:SEQ], (U0["w2"] + v) % HL, s, f_hi[:, k, :], f_lo[:, k, :], k == 0, k == F2C - 1)
                mm.then_inc(pe_units, 1)
            stats((acc_done, 53), acc, dst=banks[0])

        @block.scalar
        def _(act):
            def split(name, i, j):
                at = U0[name] + j + HI_LEAD
                if isinstance(i, int) and (8 * i + at >= N_UNITS or 8 * i + at in NATIVE):
                    return
                slot = (at // 2) % RAW
                act.wait_ge(landed[slot], 16 * i + 16 * (at // 8 + 1))
                if not isinstance(i, int) or 8 * i + at >= HL:
                    act.wait_ge(pe_units, 8 * i + at - HL + 1)
                act.activation(w_hi[:, at % HL, :], raw[:, slot, (at % 2) * UT * P:(at % 2 + 1) * UT * P],
                               ACT.Copy).then_inc(hi_done, 1)

            def mod_copy(q, s):
                act.wait_ge(mod_rows, q + 1)
                if not isinstance(q, int) or q >= 2:
                    act.wait_ge(mod_cols, q - 1)
                row_bank = row_banks[q % 2 if isinstance(q, int) and q < MOD_FIRST else 0]
                act.activation(mod_row[:, s, :], row_bank[:, 0:SEQ], ACT.Copy).then_inc(mod_copied, 1)

            def mod_piece(i, j, base):
                if j % 4 == 2:
                    mod_copy(2 * i + (MOD_FIRST + base + j // 4), j // 4)

            def root(n):
                act.wait_ge(var_done, n)
                act.activation(newt[:, 0, :], var[:], ACT.Sqrt).then_inc(root_done, 1)

            act.wait_ge(x_in_s, 16)
            act.activation(h_pad[:, :, 16:], x[:], ACT.Square).then_inc(x_sq, 1)
            act.wait_ge(vec_in, 16)
            act.wait_ge(consts, 1)
            act.activation(cz[:, :, 0:1], vec[:, VEC["c"]:VEC["c"] + DC].rearrange("p (c a) -> p c a", a=1),
                           ACT.Silu).then_inc(c_act, 1)
            act.activation(sp[:, 0, :], col("lam", 0, RC), ACT.Abs).then_inc(c_act, 1)
            act.wait_ge(c_act, 2)
            act.activation(sp[:, 1, :], sp[:, 0, :], ACT.Exp, scale=-1.0).then_inc(c_act, 1)
            root(1)
            for q in range(8):
                mod_copy(q, q % 2)
            act.wait_ge(xr_done, 1)
            act.wait_ge(gain_done, 1)
            act.wait_ge(mod_read, 2)
            for m in range(DC):
                act.activation(h_pad[:, m, 16:], h_pad[:, m, 16:], ACT.Identity, bias=modv[:, 8 * SH1 + m:8 * SH1 + m + 1],
                               scale=gain[:, 0, m:m + 1]).then_inc(h_done, 1)
                if m == 5:
                    mod_copy(8, 0)
            mod_copy(9, 1)
            for v in (-4, -3):
                split("pool", 0, v)
            for q in range(10, MOD_POOL):
                mod_copy(q, q % 2)

            def res_square(name, n, i, j, gains):
                m = 2 * i + j
                act.wait_ge(tile_read, 2 * i + (T0[name] + j + 1))
                if gains is not None:
                    act.activation(chunk(xg_hi, m), chunk(x, m), ACT.Copy, scale=gains(m)).then_inc(xg_hi_done, 1)
                if name == "down1":
                    act.activation(sq[:, 0, :], chunk(x, m), ACT.Square)
                    act.activation(sq[:, 1, :], chunk(x, m), ACT.Square, scale=col_at("norm_final", m)).then_inc(sq_done, 1)
                else:
                    act.activation(sq[:, j % 2, :], chunk(x, m), ACT.Square).then_inc(sq_done, 1)

            def col_at(name, m):
                return vec[:, bass.ds(m + VEC[name], 1)] if not isinstance(m, int) else col(name, m)

            def gain_at(n):
                return lambda m: gain[:, n, one(m)]

            act.wait_ge(gain_done, 2)
            for m in range(DC):
                act.wait_ge(tile_read, m + 1)
                if m >= 2:
                    act.wait_ge(acc_done, m - 1)
                act.activation(xg_hi[:, m, 0:SEQ], x[:, m, :], ACT.Copy, scale=gain[:, 1, m:m + 1]).then_inc(xg_hi_done, 1)
                act.activation(sq[:, m % 2, :], x[:, m, :], ACT.Square).then_inc(sq_done, 1)
                if m in (3, 4, 6, 7):
                    q = MOD_POOL + (3, 4, 6, 7).index(m)
                    mod_copy(q, q % 2)
            for v in (-2, -1, 0, 1):
                split("pool", 0, v)

            def up(name, i, j):
                act.wait_ge(tile_read, 8 * i + (T0[name] + j + 1))
                base = 0 if name == "up0" else 32
                act.activation(ub[:, j % 2, :], ab[:, j % 2, 0:SEQ], ACT.Relu, bias=ab[:, j % 2, SEQ:SEQ + 1]).then_inc(relu_done, 1)
                act.wait_ge(relu_done, 8 * i + (base + j + 1))
                act.activation(sb2[:, j % 2, :], ub[:, j % 2, :], ACT.Square).then_inc(sq2_done, 1)
                if name == "up0":
                    mod_piece(i, j, 0)
                split(name, i, j)

            def up_phase(name, n):
                for j in range(8):
                    if j == 0:
                        root(n)
                    up(name, 0, j)
                act.preload_act_table(ACT.Relu)
                with act.Fori(1, 4) as i:
                    for j in range(8):
                        up(name, i, j)

            def down(name, i, j, n, gains):
                if j % 4 == 3:
                    res_square(name, n, i, j // 4, gains)
                if name == "down0":
                    mod_piece(i, j, 8)
                split(name, i, j)

            up_phase("up0", 2)
            act.wait_ge(gain_done, 3)
            loop_units(act, "down0", lambda i, j: down("down0", i, j, 1, gain_at(2)))

            def exps(a, e):
                act.wait_ge(neg_done, 2 * a + e + 1)
                act.activation(prob[:, e, 0:128], logit[:, e, 0:128], ACT.Exp, bias=smx[:, e, 2:3], accum_out=smx[:, e, 4:5])
                act.activation(prob[:, e, 128:384], logit[:, e, 128:384], ACT.Exp, bias=smx[:, e, 3:4],
                               accum_out=smx[:, e, 5:6]).then_inc(exp_done, 1)

            def copy_pt(a, e):
                act.wait_ge(pt_done, 2 * a + e + 1)
                if a:
                    act.wait_ge(pv_done, a)
                act.activation(pT[:, e, :], t_bank[:, 0:384], ACT.Copy).then_inc(pt_copied, 1)

            for j in range(DC + 2):
                a = j - 1
                for part in range(3):
                    v = 3 * j + part
                    if j < DC:
                        if v == 0:
                            root(3)
                        act.wait_ge(tile_read, T0["qkv"] + v + 1)
                        if j >= 2:
                            if part < 2:
                                act.wait_ge(score_done, 2 * (j - 2) + 2)
                            else:
                                act.wait_ge(vt_done, j - 1)
                        act.activation(reverse(qT[:, j % 2, :]) if part == 0 else (kT, vT)[part - 1][:, j % 2, :],
                                       ab[:, v % 2, 0:SEQ].rearrange("p (b n) -> p b n", b=2) if part == 0 else ab[:, v % 2, 0:SEQ], ACT.Identity,
                                       bias=ab[:, v % 2, SEQ:SEQ + 1]).then_inc(qkv_done, 1)
                    if part == 0:
                        if j < DC:
                            mod_copy(36 + j, j % 2)
                        if 1 <= a <= DC:
                            copy_pt(a - 1, 1)
                        if j == DC:
                            mod_copy(36 + j, j % 2)
                        if 0 <= a < DC:
                            exps(a, 0)
                    if part == 1 and 0 <= a < DC:
                        exps(a, 1)
                    if part == 2:
                        if 1 <= a <= DC:
                            act.wait_ge(pv_done, a)
                            act.activation(o_hi[:, a - 1, :].rearrange("p (b n) -> p b n", b=2), reverse(o_bank[:, 0:SEQ]), ACT.Copy).then_inc(o_hi_done, 1)
                        if 0 <= a < DC:
                            copy_pt(a, 0)
                    if j < DC:
                        split("qkv", v // 8, v % 8)

            act.wait_ge(gain_done, 4)
            for j in range(8):
                if j % 2 == 0 and j < 6:
                    mod_copy(45 + j // 2, (j // 2 + 1) % 2)
                res_square("o", 2, 0, j, gain_at(3))
                split("o", 0, j)
            up_phase("up1", 4)
            loop_units(act, "down1", lambda i, j: down("down1", i, j, 3, lambda m: gain1[:, one(m)]))

            def activate(name, n, k, dst, func, b):
                act.wait_ge(tile_read, T0[name] + n + 1)
                act.activation(dst, ab[:, n % 2, 0:SEQ], func, bias=col("b_in", b)).then_inc(z_done, 1)

            def activate_psum(name, n, dst, func, b):
                act.wait_ge(pe_units, U0[name] + n + 1)
                act.activation(dst, out_bank(name, n)[:, 0:SEQ], func, bias=col("b_in", b)).then_inc(act_read, 1)

            def xb_high(m):
                act.wait_ge(xb_done, m + 1)
                act.activation(act_hi[:, m, :], rx[:, m, RTAPS - 1:], ACT.Copy).then_inc(act_hi_done, 1)

            def first_tap(m):
                act.wait_ge(u_done, m + 1)
                act.activation(y[:, m, :], u[:, m, 0:SEQ], ACT.Identity, bias=col("dw_b", m), scale=col("dw_w", m)).then_inc(ytap_done, 1)

            def recurrent_first(m):
                if m >= 2:
                    act.wait_ge(xb_done, m - 1)
                act.wait_ge(z_done, 8 + m + 1)
                act.activation(newt[:, m % 2, :], rx[:, m, 0:SEQ], ACT.Identity, bias=col("rb", m), scale=col("rw", m)).then_inc(rtap_done, 1)

            for v in range(16):
                m = v // 2
                if v == 0:
                    root(5)
                if v == 8:
                    root(6)
                if v == 1:
                    act.wait_ge(pads, 2)
                if v % 2 == 1:
                    if m >= 2:
                        act.wait_ge(u_done, m - 1)
                    if v < GLU_SPLIT:
                        act.wait_ge(tile_read, T0["glu"] + v + 1)
                        src = ab[:, 1, 0:SEQ]
                    else:
                        act.wait_ge(pe_units, U0["glu"] + v + 1)
                        src = out_bank("glu", v)[:, 0:SEQ]
                    act.activation(sq[:, m % 2, :], src, ACT.Sigmoid, bias=col("b_in", v)).then_inc(z_done, 1)
                elif m >= 1:
                    first_tap(m - 1)
                split("glu", v // 8, v % 8)
            for v in range(10):
                activate("rx", v, v, rx[:, v, RTAPS - 1:], ACT.Identity, 16 + v)
                if v == 0:
                    first_tap(7)
                for m in range(RC):
                    if REC_AT[m] == v:
                        recurrent_first(m)
                    if REC_AT[m] == v - 1:
                        xb_high(m)
                split("rx", v // 8, v % 8)
            act.wait_ge(pe_units, U0["rg"])
            act.activation(h32b[:, :, 0:SEQ], h32[:], ACT.Copy).then_inc(h32_moved, 1)
            for v in range(10, 20):
                for m in range(RC):
                    if REC_AT[m] == v:
                        recurrent_first(m)
                    if REC_AT[m] == v - 1:
                        xb_high(m)
                activate_psum("rg", v - 10, grg[:, v - 10, :], ACT.Gelu_apprx_tanh, 26 + v - 10)
                split("rg", (v - 10) // 8, (v - 10) % 8)
            g = 0
            for v in range(GATE_UNITS):
                while g < 20 and GATE_DONE[g] == v:
                    m, which = g // 2, g % 2
                    act.wait_ge(pe_units, U0["gates"] + v + 1)
                    act.activation((rt, ig)[which][:, m, :], out_bank("gates", g)[:, 0:SEQ], ACT.Sigmoid,
                                   bias=col(("ba", "bx")[which], m)).then_inc(act_read, 1)
                    g += 1
                split("gates", 0, v)
            act.wait_ge(act_read, A0["gates"] + 20)
            for m in range(RC):
                act.activation(av[:, m, :], rt[:, m, :], ACT.Exp, scale=sp[:, 6, m:m + 1]).then_inc(decay_done, 1)
            act.wait_ge(decay_done, RC)
            act.wait_ge(pe_units, U0["gb"])
            act.activation(a2[:], av[:], ACT.Square)
            for m in range(RC):
                act.activation(rt[:, m, :], rt[:, m, :], ACT.Tanh, scale=sp[:, 7, m:m + 1]).then_inc(decay_done, 1)
            for v in range(8):
                activate_psum("gb", v, sgb[:, v, :], ACT.Sigmoid, 44 + v)
                if v == MULT_AT + 1:
                    act.wait_ge(mult2_done, 1)
                    act.activation(rt[:], rt[:], ACT.Sqrt).then_inc(mult_done, 1)
                split("gb", 0, v)

            for v in range(8):
                activate_psum("ga", v, sga[:, v, :], ACT.Sigmoid, 36 + v)
            def ln_activate(m):
                act.activation(y[:, m, :], y[:, m, :], ACT.Silu, bias=col("ln_b", m), scale=col("ln_g", m)).then_inc(ln_silu, 1)
                act.wait_ge(ln_silu, m + 1)
                act.activation(xg_hi[:, m, 0:SEQ], y[:, m, :], ACT.Copy).then_inc(ln_hi, 1)

            for v in range(10):
                if v == 1:
                    act.wait_ge(ln_c, 1)
                    act.activation(u[:, :, 0:SEQ], y[:], ACT.Square).then_inc(ln_sq, 1)
                if v == 3:
                    root(7)
                if v == 5:
                    act.wait_ge(ln_n, 1)
                split("lru", v // 8, v % 8)
                if v < 5 or v == 9:
                    continue
                for m in (2 * v - 10, 2 * v - 9):
                    ln_activate(m)

            for m in range(8):
                split("conv", 0, m)
                act.wait_ge(m_done, m + 1)
                act.activation(act_hi[:, m, :], sga[:, m, :], ACT.Copy).then_inc(act_hi_done, 1)
            for m in range(8):
                res_square("mix", 4, 0, m, lambda m: col("norm2", m))
                split("mix", 0, m)

            def ffn(i, j):
                if j % 2 == 0:
                    act.wait_ge(tile_read, 8 * i + (T0["ffn"] + j + 1))
                    act.activation(sq[:, (j // 2) % 2, :], ab[:, 0, 0:SEQ], ACT.Silu).then_inc(f_silu, 1)
                split("ffn", i, j)

            for j in range(8):
                if j == 0:
                    root(8)
                ffn(0, j)
            act.preload_act_table(ACT.Silu)
            with act.Fori(1, 5) as i:
                for j in range(8):
                    ffn(i, j)
            for j in range(4):
                ffn(5, j)
            for v in range(22):
                for m in W2_DONE.get(v, ()):
                    res_square("w2", 5, 0, m, None)
                split("w2", v // 8, v % 8)
            root(9)

        @block.vector
        def _(ve):
            chain = [0]

            def link(ins):
                chain[0] += 1
                ins.then_inc(dve, 1)
                ve.wait_ge(dve, chain[0])

            def split(name, i, j):
                at = U0[name] + j + LO_LEAD
                if isinstance(i, int) and (8 * i + at >= N_UNITS or 8 * i + at in NATIVE):
                    return
                slot = (at // 2) % RAW
                ve.wait_ge(hi_done, count_of(name, i, j + LO_LEAD))
                ve.tensor_tensor(w_lo[:, at % HL, :], raw[:, slot, (at % 2) * UT * P:(at % 2 + 1) * UT * P],
                                 w_hi[:, at % HL, :].bitcast(F32), ALU.subtract).then_inc(lo_done, 1)

            def rsqrt(n, dst):
                ve.wait_ge(root_done, n)
                link(ve.reciprocal(newt[:, 1, :], newt[:, 0, :]))
                link(ve.tensor_tensor(newt[:, 0, :], newt[:, 1, :], newt[:, 1, :], ALU.mult))
                link(ve.tensor_tensor(newt[:, 0, :], newt[:, 0, :], var[:], ALU.mult))
                link(ve.tensor_scalar(newt[:, 0, :], newt[:, 0, :], -0.5, 1.5, ALU.mult, ALU.add))
                link(ve.tensor_tensor(dst, newt[:, 1, :], newt[:, 0, :], ALU.mult))

            def variance(n, nv, src):
                ve.wait_ge(stat_mm, n)
                ve.tensor_scalar(var[:], src[:, 0:SEQ], 1.0 / D, EPS, ALU.mult, ALU.add).then_inc(var_done, 1)

            def norm(n, nv, dst, src=stat_bank):
                variance(n, nv, src)
                rsqrt(nv, dst)

            def over_chunks(t):
                return t.rearrange("p c t -> p t c")

            def mod_group(g):
                ve.wait_ge(mod_cols, 4 * g + 4)
                ve.tensor_tensor(modv[:, 8 * g:8 * g + 8], col_banks[g % 2][:, 0:8], col("b_mod", 8 * g, 8), ALU.add).then_inc(mod_read, 1)
                ve.wait_ge(mod_read, g + 1)

            def mod_two(q):
                ve.wait_ge(mod_cols, q + 1)
                c = 2 * q
                ve.tensor_tensor(modv[:, bass.ds(c, 2)], col_banks[0][:, 0:2], vec[:, bass.ds(c + VEC["b_mod"], 2)], ALU.add).then_inc(mod_read, 1)

            def mod_two_at(i, j, base):
                if j % 4 == 3:
                    mod_two(2 * i + (MOD_FIRST + base + j // 4))

            def make_gain(n, sc, norm_col):
                ve.scalar_tensor_tensor(gain[:, n, :], modv[:, sc:sc + DC], 1.0, norm_col, ALU.add, ALU.mult).then_inc(gain_done, 1)

            def shift(at):
                src = modv[:, at:at + DC].rearrange("p (c a) -> p c a", a=1).broadcast_to((P, DC, 2))
                link(ve.tensor_copy(xg_hi[:, :, SEQ:SEQ + 2], src))
                ve.tensor_tensor(xg_lo[:, :, SEQ:SEQ + 2], src, xg_hi[:, :, SEQ:SEQ + 2].bitcast(F32), ALU.subtract).then_inc(shift_done, 1)

            ve.wait_ge(x_sq, 1)
            ve.tensor_reduce(acc[:], over_chunks(h_pad[:, :, 16:]), AX.X, ALU.add).then_inc(stat_in, 1)
            ve.wait_ge(vec_in, 16)
            ve.wait_ge(c_act, 3)
            link(ve.tensor_scalar(sp[:, 2, :], sp[:, 1, :], 2.0, None, ALU.add))
            link(ve.reciprocal(sp[:, 3, :], sp[:, 2, :]))
            link(ve.tensor_tensor(sp[:, 2, :], sp[:, 1, :], sp[:, 3, :], ALU.mult))
            link(ve.tensor_tensor(sp[:, 3, :], sp[:, 2, :], sp[:, 2, :], ALU.mult))
            link(ve.tensor_scalar(sp[:, 4, :], sp[:, 3, :], 1.0 / 17, 1.0 / 15, ALU.mult, ALU.add))
            for k in (13, 11, 9, 7, 5, 3, 1):
                link(ve.tensor_tensor(sp[:, 4, :], sp[:, 4, :], sp[:, 3, :], ALU.mult))
                link(ve.tensor_scalar(sp[:, 4, :], sp[:, 4, :], 1.0 / k, None, ALU.add))
            link(ve.scalar_tensor_tensor(sp[:, 5, :], sp[:, 4, :], 2.0, sp[:, 2, :], ALU.mult, ALU.mult))
            link(ve.tensor_scalar(sp[:, 4, :], col("lam", 0, RC), -1.0, 0.0, ALU.mult, ALU.max))
            link(ve.tensor_tensor(sp[:, 5, :], sp[:, 5, :], sp[:, 4, :], ALU.add))
            link(ve.tensor_scalar(sp[:, 6, :], sp[:, 5, :], -8.0, None, ALU.mult))
            link(ve.tensor_scalar(sp[:, 7, :], sp[:, 5, :], 8.0, None, ALU.mult))
            link(ve.tensor_tensor(gain1[:], col("norm_final", 0, DC), col("norm1", 0, DC), ALU.mult))
            norm(1, 1, rstd[:, 0:SEQ])
            ve.tensor_tensor(h_pad[:, :, 16:], x[:], rstd[:, 0:SEQ].rearrange("p (a n) -> p a n", a=1).broadcast_to((P, DC, SEQ)),
                             ALU.mult).then_inc(xr_done, 1)
            ve.wait_ge(bias_mm, 1)
            ve.tensor_copy(bydist[:], banks[0][0:HEADS, 0:384]).then_inc(bias_cp, 1)
            mod_group(0)
            make_gain(0, 8 * SC1, col("norm_mix", 0, DC))
            mod_group(1)

            ve.wait_ge(h_done, DC)
            ve.wait_ge(consts, 8)
            ve.wait_ge(inv_in, 16)
            W = slice(16, 16 + SEQ)
            link(ve.tensor_tensor(s2[:, :, W], h_pad[:, :, W], h_pad[:, :, 15:15 + SEQ], ALU.add))
            link(ve.tensor_tensor(s4[:, :, W], s2[:, 2:8, W], s2[:, 2:8, 14:14 + SEQ], ALU.add))
            link(ve.tensor_tensor(s8[:, :, W], s4[:, 2:6, W], s4[:, 2:6, 12:12 + SEQ], ALU.add))
            link(ve.tensor_tensor(s16[:, :, W], s8[:, 2:4, W], s8[:, 2:4, 8:8 + SEQ], ALU.add))
            for g, t in enumerate((s2, s4, s8, s16)):
                part = t[:, 0:2, W]
                link(ve.tensor_tensor(part, part, invc[:, g:g + 1, :].broadcast_to((P, 2, SEQ)), ALU.mult))
                link(ve.tensor_tensor(part, part, h_pad[:, 2 * g:2 * g + 2, W], ALU.subtract))
                link(ve.tensor_copy(pool_hi[:, 2 * g:2 * g + 2, :], part))
                ve.tensor_tensor(pool_lo[:, 2 * g:2 * g + 2, :], part, pool_hi[:, 2 * g:2 * g + 2, :].bitcast(F32),
                                 ALU.subtract).then_inc(pool_in, 1)
            mod_group(2)
            link(ve.tensor_tensor(gate0[:], modv[:, 8 * G1:8 * G1 + DC], col("pool_scale", 0, DC), ALU.mult))
            for v in (-3, -2):
                split("pool", 0, v)
            mod_group(3)
            make_gain(1, 8 * SC2, col("norm_mlp", 0, DC))
            ve.wait_ge(gain_done, 2)

            def pool_finish(m):
                ve.wait_ge(xg_hi_done, m + 1)
                ve.scalar_tensor_tensor(xg_lo[:, m, 0:SEQ], x[:, m, :], gain[:, 1, m:m + 1], xg_hi[:, m, 0:SEQ].bitcast(F32),
                                        ALU.mult, ALU.subtract).then_inc(xg_lo_done, 1)
                ve.wait_ge(sq_done, m + 1)
                if m:
                    ve.wait_ge(acc_done, m)
                    ve.tensor_tensor(acc[:], acc[:], sq[:, m % 2, :], ALU.add).then_inc(acc_done, 1)
                else:
                    ve.tensor_copy(acc[:], sq[:, 0, :]).then_inc(acc_done, 1)

            for m in range(DC):
                if m % 4 == 0:
                    ve.wait_ge(pe_units, m // 4 + 1)
                ve.scalar_tensor_tensor(x[:, m, :], out_bank("pool", m)[:, 0:SEQ], gate0[:, m:m + 1], x[:, m, :], ALU.mult,
                                        ALU.add).then_inc(tile_read, 1)
                if m >= 2:
                    pool_finish(m - 2)
            for m in (DC - 2, DC - 1):
                pool_finish(m)
            mod_group(4)
            shift(8 * SH2)
            for v in (-1, 0, 1):
                split("pool", 0, v)

            def up(name, i, j):
                base = 0 if name == "up0" else 32
                ve.wait_ge(pe_units, 8 * i + (U0[name] + j + 1))
                ve.tensor_tensor(ab[:, j % 2, :], out_bank(name, j)[:, 0:SEQ + 2], rstd[:], ALU.mult).then_inc(tile_read, 1)
                split(name, i, j)
                t = 8 * i + j
                ve.wait_ge(sq2_done, 8 * i + (base + j + 1))
                ve.tensor_copy(chunk(hid_hi, t), sb2[:, j % 2, :]).then_inc(hid_hi_done, 1)
                ve.wait_ge(hid_hi_done, 8 * i + (base + j + 1))
                ve.tensor_tensor(chunk(hid_lo, t), sb2[:, j % 2, :], chunk(hid_hi, t).bitcast(F32),
                                 ALU.subtract).then_inc(hid_lo_done, 1)
                if name == "up0":
                    mod_two_at(i, j, 0)

            def up_phase(name, n):
                norm(n, n, rstd[:, 0:SEQ])
                for j in range(8):
                    up(name, 0, j)
                with ve.Fori(1, 4) as i:
                    for j in range(8):
                        up(name, i, j)

            def clear(two=False):
                ve.memset(acc[:], 0.0).then_inc(acc_done, 1)
                if two:
                    ve.memset(acc2[:], 0.0).then_inc(acc2_done, 1)

            def residual(name, i, j, gate):
                m = 2 * i + j
                dst, src = chunk(x, m), out_bank(name, j)[:, 0:SEQ]
                if gate is None:
                    ve.tensor_tensor(dst, src, dst, ALU.add).then_inc(tile_read, 1)
                else:
                    g = modv[:, gate + m:gate + m + 1] if isinstance(m, int) else modv[:, bass.ds(m + gate, 1)]
                    ve.scalar_tensor_tensor(dst, src, g, dst, ALU.mult, ALU.add).then_inc(tile_read, 1)

            def finish(name, n, i, j, gains):
                m = 2 * i + j
                if gains is not None:
                    ve.wait_ge(xg_hi_done, 2 * i + (8 * n + j + 1))
                    src = xg_hi[:, one(m), 0:SEQ].rearrange("p a n -> p (a n)")
                    dst = xg_lo[:, one(m), 0:SEQ].rearrange("p a n -> p (a n)")
                    ve.scalar_tensor_tensor(dst, chunk(x, m), gains(m), src.bitcast(F32), ALU.mult, ALU.subtract)\
                        .then_inc(xg_lo_done, 1)
                ve.wait_ge(sq_done, 2 * i + (8 * n + j + 1))
                ve.wait_ge(acc_done, 2 * i + (9 * n + j))
                if name == "down1":
                    ve.wait_ge(acc2_done, 2 * i + (j + 1))
                    ve.tensor_tensor(acc2[:], acc2[:], sq[:, 1, :], ALU.add).then_inc(acc2_done, 1)
                ve.tensor_tensor(acc[:], acc[:], sq[:, 0 if name == "down1" else j % 2, :], ALU.add).then_inc(acc_done, 1)

            def down(name, n, i, j, gate, gains):
                if j % 4 < 3:
                    split(name, i, j)
                else:
                    ve.wait_ge(pe_units, 8 * i + (U0[name] + j + 1))
                    residual(name, i, j // 4, gate)
                    split(name, i, j)
                    finish(name, n, i, j // 4, gains)
                if name == "down0":
                    mod_two_at(i, j, 8)

            up_phase("up0", 2)
            ve.wait_ge(mod_read, 13)
            make_gain(2, 48 + 8 * SC1, col("norm_mix", 8, DC))
            ve.wait_ge(gain_done, 3)
            clear()
            with ve.Fori(0, 3) as i:
                for j in range(8):
                    down("down0", 1, i, j, 8 * G2, lambda m: gain[:, 2, one(m)])
            ve.wait_ge(mod_read, 17)
            shift(48 + 8 * SH1)
            for j in range(8):
                down("down0", 1, 3, j, 8 * G2, lambda m: gain[:, 2, one(m)])

            def logits(a, e):
                h = 2 * a + e
                ve.wait_ge(toep_in[a % 2], 32 * (a // 2 + 1))
                ve.wait_ge(score_done, h + 1)
                ve.scalar_tensor_tensor(logit[:, e, :], s_bank[:, 0:384], float(HD) ** -0.5, toep[:, a % 2, e, :],
                                        ALU.mult, ALU.add).then_inc(logit_done, 1)
                ve.wait_ge(logit_done, h + 1)
                ve.tensor_reduce(smx[:, e, 0:1], logit[:, e, 0:128], AX.X, ALU.max)
                ve.tensor_reduce(smx[:, e, 1:2], logit[:, e, 128:384], AX.X, ALU.max).then_inc(max_done, 1)
                ve.wait_ge(max_done, h + 1)
                ve.tensor_scalar(smx[:, e, 2:4], smx[:, e, 0:2], -1.0, None, ALU.mult).then_inc(neg_done, 1)

            def normalize(a, e):
                ve.wait_ge(exp_done, 2 * a + e + 1)
                link(ve.reciprocal(smx[:, e, 6:8], smx[:, e, 4:6]))
                ve.tensor_scalar(probn[:, e, 0:128], prob[:, e, 0:128], smx[:, e, 6:7], None, ALU.mult)
                ve.tensor_scalar(probn[:, e, 128:384], prob[:, e, 128:384], smx[:, e, 7:8], None, ALU.mult).then_inc(prob_done, 1)

            for j in range(DC + 2):
                a = j - 1
                for part in range(3):
                    v = 3 * j + part
                    if part == 2 and 0 <= a < DC:
                        ve.wait_ge(vt_done, a + 1)
                        ve.tensor_copy(vtok[:, a % 2, :], t_bank[:, 0:256]).then_inc(vt_copied, 1)
                    if j < DC:
                        if v == 0:
                            norm(3, 3, rstd[:, 0:SEQ])
                        ve.wait_ge(pe_units, U0["qkv"] + v + 1)
                        if v >= 2:
                            ve.wait_ge(qkv_done, v - 1)
                        ve.tensor_tensor(ab[:, v % 2, :], out_bank("qkv", v)[:, 0:SEQ + 2], rstd[:], ALU.mult).then_inc(tile_read, 1)
                        split("qkv", v // 8, v % 8)
                    if part == 0 and 0 <= a < DC:
                        logits(a, 0)
                    if part == 1:
                        if 0 <= a < DC:
                            normalize(a, 0)
                            logits(a, 1)
                        if j <= DC:
                            mod_two(36 + j)
                    if part == 2:
                        if 0 <= a < DC:
                            normalize(a, 1)
                        if 1 <= a <= DC:
                            ve.wait_ge(o_hi_done, a)
                            two = [t[:, a - 1, :].rearrange("p (b n) -> p b n", b=2) for t in (o_lo, o_hi)]
                            ve.tensor_tensor(two[0], reverse(o_bank[:, 0:SEQ]), two[1].bitcast(F32), ALU.subtract).then_inc(o_lo_done, 1)

            ve.wait_ge(mod_read, 29)
            make_gain(3, 48 + 8 * SC2, col("norm_mlp", 8, DC))
            ve.wait_ge(gain_done, 4)
            shift(48 + 8 * SH2)
            clear()
            for j in range(8):
                ve.wait_ge(pe_units, U0["o"] + j + 1)
                residual("o", 0, j, 48 + 8 * G1)
                split("o", 0, j)
                if j:
                    finish("o", 2, 0, j - 1, lambda m: gain[:, 3, one(m)])
                if j % 2 == 1 and j < 6:
                    mod_two(45 + j // 2)
            finish("o", 2, 0, 7, lambda m: gain[:, 3, one(m)])
            up_phase("up1", 4)
            ve.wait_ge(mod_read, 33)
            clear(two=True)
            loop_units(ve, "down1", lambda i, j: down("down1", 3, i, j, 48 + 8 * G2, lambda m: gain1[:, one(m)]))

            def scaled(name, v, w=SEQ):
                ve.wait_ge(pe_units, U0[name] + v + 1)
                ve.tensor_tensor(ab[:, v % 2, 0:SEQ], out_bank(name, v)[:, 0:SEQ], rstd[:, 0:SEQ], ALU.mult).then_inc(tile_read, 1)

            def recurrent_conv(m):
                ve.wait_ge(rtap_done, m + 1)
                t = newt[:, m % 2, :]
                for k in (1, 2):
                    link(ve.scalar_tensor_tensor(t, rx[:, m, k:k + SEQ], col("rw", RC * k + m), t, ALU.mult, ALU.add))
                ve.scalar_tensor_tensor(rx[:, m, 3:3 + SEQ], rx[:, m, 3:3 + SEQ], col("rw", RC * 3 + m), t, ALU.mult, ALU.add)\
                    .then_inc(xb_done, 1)

            def low(n, m, src, ready):
                ve.wait_ge(*ready)
                ve.wait_ge(act_hi_done, n + 1)
                ve.tensor_tensor(act_lo[:, m, :], src, act_hi[:, m, :].bitcast(F32), ALU.subtract).then_inc(act_lo_done, 1)

            def xb_low(m):
                low(m, m, rx[:, m, 3:3 + SEQ], (xb_done, m + 1))

            def taps(n0, n1):
                for n in range(n0, min(n1, LAST_TAPS)):
                    pair, k, m = n // (2 * (TAPS - 1)), n % (2 * (TAPS - 1)) // 2 + 1, n % 2
                    m += 2 * pair
                    if k == 1:
                        ve.wait_ge(ytap_done, m + 1)
                    else:
                        ve.wait_ge(tap_done, n - 1)
                    ve.scalar_tensor_tensor(y[:, m, :], u[:, m, k:k + SEQ], col("dw_w", DC * k + m), y[:, m, :], ALU.mult, ALU.add)\
                        .then_inc(tap_done, 1)

            done = [0]

            def more_taps(n):
                taps(done[0], done[0] + n)
                done[0] += n

            for v in range(16):
                m = v // 2
                if v == 0:
                    ve.wait_ge(stat_mm, 6)
                    link(ve.tensor_scalar(acc2[:], stat_bank[:, 0:SEQ], 1.0 / D, EPS, ALU.mult, ALU.add))
                    link(ve.tensor_scalar(newt[:, 1, :], acc2[:], EPS, None, ALU.mult))
                    ve.scalar_tensor_tensor(var[:], stat_bank[:, SEQ:2 * SEQ], 1.0 / D, newt[:, 1, :], ALU.mult, ALU.add)\
                        .then_inc(var_done, 1)
                    rsqrt(5, rstd[:, 0:SEQ])
                if v == 8:
                    ve.tensor_copy(var[:], acc2[:]).then_inc(var_done, 1)
                if v == 9:
                    rsqrt(6, rstd1[:])
                if v < GLU_SPLIT:
                    if v >= 2 and v % 2 == 0:
                        ve.wait_ge(u_done, m)
                    elif v >= 2:
                        ve.wait_ge(z_done, m)
                    scaled("glu", v)
                split("glu", v // 8, v % 8)
                if v < 8:
                    ve.scalar_tensor_tensor(h32[:, v, :], x[:, v, :], gain1[:, v:v + 1], rstd[:, 0:SEQ], ALU.mult, ALU.mult).then_inc(h32_done, 1)
                if v % 2 == 1:
                    ve.wait_ge(z_done, m + 1)
                    if v == 1:
                        ve.wait_ge(pads, 2)
                    src = ab[:, 0, 0:SEQ] if v < GLU_SPLIT else out_bank("glu", v - 1)[:, 0:SEQ]
                    ve.scalar_tensor_tensor(u[:, m, TAPS - 1:], src, col("b_in", v - 1), sq[:, m % 2, :],
                                            ALU.add, ALU.mult).then_inc(u_done, 1)
                more_taps(TAPS_AT["glu"][v])
            for v in range(20):
                if v < 10:
                    ve.wait_ge(z_done, 8 + max(v - 1, 0))
                    scaled("rx", v)
                    split("rx", v // 8, v % 8)
                else:
                    split("rg", (v - 10) // 8, (v - 10) % 8)
                for m in range(RC):
                    if REC_AT[m] == v - 1:
                        xb_low(m)
                for m in range(RC):
                    if REC_AT[m] == v:
                        recurrent_conv(m)
                more_taps(TAPS_AT["rx"][v])
            for v in range(GATE_UNITS):
                split("gates", 0, v)
                more_taps(TAPS_AT["gates"][v])

            def recurrence(m):
                link(ve.tensor_tensor_scan(rt[:, m, :], av[:, m, :], ig[:, m, :], 0.0, ALU.mult, ALU.add))
                if m % 2 == 1:
                    ve.tensor_tensor(rt[:, m - 1:m + 1, :], rt[:, m - 1:m + 1, :], grg[:, m - 1:m + 1, :], ALU.mult).then_inc(hb_done, 1)

            for v in range(16):
                if v == 0:
                    ve.wait_ge(act_read, A0["gates"] + 20)
                    link(ve.tensor_tensor(ig[:], ig[:], rx[:, :, RTAPS - 1:], ALU.mult))
                if v == MULT_AT:
                    ve.wait_ge(decay_done, 2 * RC)
                    ve.scalar_tensor_tensor(rt[:], a2[:], 1.0, rt[:], ALU.add, ALU.mult).then_inc(mult2_done, 1)
                if v == MULT_AT + 2:
                    ve.wait_ge(mult_done, 1)
                    link(ve.tensor_tensor(ig[:], ig[:], rt[:], ALU.mult))
                more_taps(TAPS_AT["gb"][v])
                for m in range(RC):
                    if HB_AT[m] == v:
                        recurrence(m)

            def layernorm_steps(v):
                if v == 0:
                    ve.wait_ge(tap_done, LAST_TAPS)
                    ve.tensor_reduce(acc2[:], over_chunks(y[:]), AX.X, ALU.add).then_inc(stat_in, 1)
                if v == 1:
                    ve.wait_ge(stat_mm, 7)
                    link(ve.tensor_scalar(newt[:, 0, :], stat_bank[:, 0:SEQ], 1.0 / D, None, ALU.mult))
                    ve.tensor_tensor(y[:], y[:], newt[:, 0:1, :].broadcast_to((P, DC, SEQ)), ALU.subtract).then_inc(ln_c, 1)
                if v in (2, 3):
                    ve.wait_ge(h32_done, DC)
                    for m in range(4 * (v - 2), 4 * (v - 2) + 4):
                        ve.scalar_tensor_tensor(x[:, m, :], x[:, m, :], col("norm_final", m), rstd1[:], ALU.mult, ALU.mult)
                if v == 2:
                    ve.wait_ge(ln_sq, 1)
                    ve.tensor_reduce(acc2[:], over_chunks(u[:, :, 0:SEQ]), AX.X, ALU.add).then_inc(stat_in, 1)
                if v == 4:
                    norm(8, 7, rstd1[:])
                    ve.tensor_tensor(y[:], y[:], rstd1[:].rearrange("p (a n) -> p a n", a=1).broadcast_to((P, DC, SEQ)),
                                     ALU.mult).then_inc(ln_n, 1)

            for v in range(10):
                split("lru", v // 8, v % 8)
                for m in range(RC):
                    if HB_AT[m] == 16 + v:
                        recurrence(m)
                for m in {5: (0, 1, 2, 3), 7: (4,), 8: (5,), 9: (6, 7)}.get(v, ()):
                    ve.wait_ge(pe_units, U0["lru"] + (5 if m < 4 else LRU_UNIT[m] + 1))
                    if m == 0:
                        ve.wait_ge(act_read, A0["ga"] + 8)
                    ve.tensor_tensor(sgb[:, m, :], out_bank("lru", m)[:, 0:SEQ], sgb[:, m, :], ALU.mult).then_inc(tile_read, 1)
                layernorm_steps(v)
                if 5 < v:
                    for m in (2 * v - 12, 2 * v - 11):
                        ve.wait_ge(ln_hi, m + 1)
                        ve.tensor_tensor(xg_lo[:, m, 0:SEQ], y[:, m, :], xg_hi[:, m, 0:SEQ].bitcast(F32), ALU.subtract).then_inc(ln_lo, 1)
            for m in range(8):
                ve.wait_ge(pe_units, U0["conv"] + m + 1)
                ve.scalar_tensor_tensor(sga[:, m, :], out_bank("conv", m)[:, 0:SEQ], col("cb", m), sga[:, m, :], ALU.add,
                                        ALU.mult).then_inc(tile_read, 1)
                split("conv", 0, m)
                if m:
                    low(RC + m - 1, m - 1, sga[:, m - 1, :], (m_done, m))
                ve.wait_ge(tile_read, T0["conv"] + m + 1)
                ve.tensor_tensor(sga[:, m, :], sga[:, m, :], sgb[:, m, :], ALU.add).then_inc(m_done, 1)
            low(RC + 7, 7, sga[:, 7, :], (m_done, 8))
            clear()
            for m in range(8):
                ve.wait_ge(pe_units, U0["mix"] + m + 1)
                residual("mix", 0, m, None)
                split("mix", 0, m)
                if m:
                    finish("mix", 4, 0, m - 1, lambda m: col("norm2", m))
            finish("mix", 4, 0, 7, lambda m: col("norm2", m))

            def ffn(i, j):
                t = 8 * i + (T0["ffn"] + j + 1)
                ve.wait_ge(pe_units, 8 * i + (U0["ffn"] + j + 1))
                ve.tensor_tensor(ab[:, j % 2, 0:SEQ], out_bank("ffn", j)[:, 0:SEQ], rstd[:, 0:SEQ], ALU.mult).then_inc(tile_read, 1)
                split("ffn", i, j)
                if j % 2 == 1:
                    m, b = 4 * i + j // 2, (j // 2) % 2
                    ve.wait_ge(tile_read, t)
                    ve.wait_ge(f_silu, m + 1)
                    ve.tensor_tensor(newt[:, b, :], ab[:, 1, 0:SEQ], sq[:, b, :], ALU.mult).then_inc(f_prod, 1)
                    ve.wait_ge(f_prod, m + 1)
                    ve.tensor_copy(chunk(f_hi, m), newt[:, b, :]).then_inc(f_hi_done, 1)
                    ve.wait_ge(f_hi_done, m + 1)
                    ve.tensor_tensor(chunk(f_lo, m), newt[:, b, :], chunk(f_hi, m).bitcast(F32), ALU.subtract).then_inc(f_lo_done, 1)

            norm(9, 8, rstd[:, 0:SEQ])
            for j in range(8):
                ffn(0, j)
            with ve.Fori(1, 5) as i:
                for j in range(8):
                    ffn(i, j)
            for j in range(4):
                ffn(5, j)
            clear()
            for v in range(22):
                split("w2", v // 8, v % 8)
                for m in W2_DONE.get(v, ()):
                    ve.wait_ge(pe_units, U0["w2"] + (11 if m < 4 else LAST_UNIT[m] + 1))
                    residual("w2", 0, m, None)
                    finish("w2", 5, 0, m, None)
            norm(10, 9, rstd[:, 0:SEQ], banks[0])
            for m in range(DC):
                ve.scalar_tensor_tensor(yout[:, m, :], x[:, m, :], col("norm_f", m), rstd[:, 0:SEQ], ALU.mult, ALU.mult)\
                    .then_inc(yout_done, 1)


def bucket_table():
    t = np.zeros((33, 384), np.float32)
    for c in range(384):
        if c > 255:
            t[32, c] = 1.0
            continue
        dist = 255 - c
        if dist < 16:
            b = dist
        else:
            b = min(16 + int(np.float32(math.log(dist / 16)) / math.log(64) * 16 + 1e-6), 31)
        t[b, c] = 1.0
    return t


def columns(a):
    return np.ascontiguousarray(a.reshape(-1, P).T)


def tiles_of(w):
    k, m = w.shape
    return w.reshape(k // P, P, m // P, P).transpose(0, 2, 1, 3)


def stream(inputs):
    units = []

    def unit(tiles):
        block = np.zeros((P, UT, P), np.float32)
        for s, t in enumerate(tiles):
            block[:, s, :] = t
        units.append(block.reshape(P, UT * P))

    def by_output(w, order=None):
        t = tiles_of(w)
        for m in (range(t.shape[1]) if order is None else order):
            for k in range(0, t.shape[0], UT):
                unit([t[k + s, m] for s in range(UT)])

    def first_half(w):
        t = tiles_of(w)
        for q in range(t.shape[0] // 2):
            unit([t[2 * q + s // 4, s % 4] for s in range(UT)])

    def one_by_one(w, order):
        t = tiles_of(w)
        for n in range(0, len(order), UT):
            unit([t[k, m] for m, k in order[n:n + UT]])

    pool = [tiles_of(inputs["w_pool"][0, g]) for g in range(4)]
    for v in range(2):
        unit([pool[m // 2][kk, m % 2] for m in range(4 * v, 4 * v + 4) for kk in range(2)])
    by_output(inputs["w_up"][0])
    by_output(inputs["w_down"][0])
    by_output(inputs["w_qkv"][0], [8 * part + j for j in range(DC) for part in range(3)])
    by_output(inputs["w_o"][0])
    by_output(inputs["w_up"][1])
    by_output(inputs["w_down"][1])
    order = {"rx": range(16, 26), "glu": [x for m in range(8) for x in (m, 8 + m)], "rg": range(26, 36),
             "gb": range(44, 52), "ga": range(36, 44)}
    for name in ("glu", "rx", "rg"):
        by_output(inputs["w_in_2"][0], order[name])
    full = []
    for name in ("lru_wa_2", "lru_wx_2"):
        w = np.zeros((RC * P, RC * P), np.float32)
        for h in range(16):
            w[80 * h:80 * h + 80, 80 * h:80 * h + 80] = inputs[name][0, h]
        full.append(tiles_of(w))
    for v in range(GATE_UNITS):
        unit([full[g[1]][g[2], g[0]] for n, g in enumerate(GATES) if GATE_AT[n][0] == v])
    for name in ("gb", "ga"):
        by_output(inputs["w_in_2"][0], order[name])
    first_half(inputs["lru_w_out_2"][0])
    one_by_one(inputs["lru_w_out_2"][0], LRU_TILES)
    by_output(inputs["conv_w_out_2"][0])
    by_output(inputs["w_mix_out_2"][0])
    w1, w3 = tiles_of(inputs["ffn_w1_2"][0]), tiles_of(inputs["ffn_w3_2"][0])
    for m in range(F2C):
        unit([w1[k, m] for k in range(DC)])
        unit([w3[k, m] for k in range(DC)])
    first_half(inputs["ffn_w2_2"][0])
    one_by_one(inputs["ffn_w2_2"][0], LAST_TILES)
    assert len(units) == N_UNITS
    return np.stack(units).reshape(N_PAIRS, 2, P, UT * P).transpose(0, 2, 1, 3).reshape(N_PAIRS, P, PAIR)


def layouts(inputs):
    b_in = columns(inputs["b_in_2"][0])
    order = [x for m in range(8) for x in (m, 8 + m)] + list(range(16, 52))
    mod = inputs["w_mod"].reshape(2, DC, P, 6, 4, 2 * P)[:, :, :, list(MOD_ORDER)]
    b_mod = inputs["b_mod"].reshape(2, 6, D)[:, list(MOD_ORDER)]
    parts = [("c", inputs["c"]), ("b_mod", b_mod), ("norm_mix", inputs["norm_mix"]), ("norm_mlp", inputs["norm_mlp"]),
             ("pool_scale", inputs["pool_scale"]), ("norm_final", inputs["norm_final"]), ("norm1", inputs["norm1_g_2"]),
             ("norm2", inputs["norm2_g_2"]), ("norm_f", inputs["norm_f_g_2"]), ("b_in", None),
             ("dw_w", inputs["conv_dw_w_2"]), ("dw_b", inputs["conv_dw_b_2"]), ("ln_g", inputs["conv_ln_g_2"]),
             ("ln_b", inputs["conv_ln_b_2"]), ("cb", inputs["conv_b_out_2"]), ("rw", inputs["lru_conv_w_2"]),
             ("rb", inputs["lru_conv_b_2"]), ("ba", inputs["lru_ba_2"]), ("bx", inputs["lru_bx_2"]),
             ("lam", inputs["lru_lambda_2"])]
    assert [p[0] for p in parts] == list(VEC)
    vectors = np.concatenate([b_in[:, order] if a is None else columns(np.asarray(a)) for _, a in parts], axis=1)
    assert vectors.shape == (P, NVEC)
    return {
        "weights": stream(inputs),
        "w_mod": np.ascontiguousarray(mod.transpose(0, 3, 4, 2, 1, 5).reshape(MODS, P, DC * SEQ)),
        "x_in": np.ascontiguousarray(inputs["x"][0].T.reshape(DC, P, SEQ).transpose(1, 0, 2)),
        "vectors": np.ascontiguousarray(vectors),
        "rel_bias": np.ascontiguousarray(inputs["rel_bias"]),
        "buckets": bucket_table(),
        "inv_count": (1.0 / np.minimum(np.arange(1, SEQ + 1)[None, :], np.array(WINDOWS)[:, None])).astype(np.float32),
        "identity": np.eye(P, dtype=np.float32),
    }


def kernel(**inputs):
    import concourse.bacc as bacc
    from concourse.bass_utils import run_bass_kernel_spmd

    inputs = {k: np.asarray(v) for k, v in inputs.items()}
    arrays = layouts(inputs)
    nc = bacc.Bacc("TRN2", target_bir_lowering=False, num_devices=1)
    args = [nc.dram_tensor(k, a.shape, mybir.dt.from_np(a.dtype), kind="ExternalInput").ap() for k, a in arrays.items()]
    out = nc.dram_tensor("y_out", (D, SEQ), F32, kind="ExternalOutput").ap()
    build(nc, *args, out)
    got = run_bass_kernel_spmd(nc, [arrays], core_ids=[0]).results[0]["y_out"]
    return np.ascontiguousarray(np.asarray(got).T)[None]
```
